# Optimizing a Trainium2 kernel written in Bass

```python
import jax, jax.numpy as jnp
from jax import lax
import numpy as np
import math
import jax
import jax.numpy as jnp

D_MODEL = 2048
BATCH = 1
SEQ = 512
DEPTH = 1

GRID_W = 64
CTX_LEN = 256
Q_BLOCK = 128
HEAD_DIM = 128
BRANCH_W = 512
N_BRANCHES = 4
MIX_W = N_BRANCHES * BRANCH_W
A_HEADS = 4
A_KV_HEADS = 2
B_HEADS = 4
NA_KH = 8
NA_KW = 16
C_HEADS = 4
C_KV_HEADS = 2
WINDOW = 128
D_HEADS = 4
MLA_KV_RANK = 512
MLA_NOPE = 128
MLA_ROPE = 64
MLA_V = 128
MLA_QK = MLA_NOPE + MLA_ROPE
ROPE_THETA = 10000.0
EPS = 1e-6
IN_SPLITS = (
    A_HEADS * HEAD_DIM, A_KV_HEADS * HEAD_DIM, A_KV_HEADS * HEAD_DIM, BRANCH_W,
    B_HEADS * HEAD_DIM, B_HEADS * HEAD_DIM, B_HEADS * HEAD_DIM, BRANCH_W,
    C_HEADS * HEAD_DIM, C_KV_HEADS * HEAD_DIM, C_KV_HEADS * HEAD_DIM, BRANCH_W,
    D_HEADS * MLA_QK, MLA_KV_RANK, MLA_ROPE, BRANCH_W,
)
IN_COLS = sum(IN_SPLITS)


def rms_norm(x, g):
    xf = x.astype(jnp.float32)
    y = xf * lax.rsqrt(jnp.mean(xf * xf, axis=-1, keepdims=True) + EPS)
    return (y * g.astype(jnp.float32)).astype(x.dtype)

def heads(t, n):
    return t.reshape(t.shape[:-1] + (n, t.shape[-1] // n))

def split_cols(y):
    return jnp.split(y, np.cumsum(IN_SPLITS)[:-1].tolist(), axis=-1)

def axial_rope_tables(n_tokens, rot_dim):
    t = jnp.arange(n_tokens)
    row = (t // GRID_W).astype(jnp.float32)
    col = (t % GRID_W).astype(jnp.float32)
    n_freq = rot_dim // 4
    inv_freq = ROPE_THETA ** (-jnp.arange(n_freq, dtype=jnp.float32) / n_freq)
    ang = jnp.concatenate([row[:, None] * inv_freq, col[:, None] * inv_freq], axis=-1)
    return jnp.cos(ang), jnp.sin(ang)

def apply_rope(x, cos, sin):
    x1, x2 = jnp.split(x.astype(jnp.float32), 2, axis=-1)
    cs, sn = cos[None, :, None, :], sin[None, :, None, :]
    return jnp.concatenate([x1 * cs - x2 * sn, x1 * sn + x2 * cs], axis=-1).astype(x.dtype)

def softmax_with_sink(s, sink):
    if sink is None:
        return jax.nn.softmax(s, axis=-1)
    sk = sink.astype(jnp.float32).reshape(s.shape[1], s.shape[2], 1, 1)
    m = jnp.maximum(jnp.max(s, axis=-1, keepdims=True), sk)
    e = jnp.exp(s - m)
    return e / (jnp.sum(e, axis=-1, keepdims=True) + jnp.exp(sk - m))

def to_blocks(q):
    B, S = q.shape[:2]
    return q.reshape((B, S // Q_BLOCK, Q_BLOCK) + q.shape[2:]).swapaxes(0, 1)

def from_blocks(o):
    o = o.swapaxes(0, 1)
    return o.reshape(o.shape[0], o.shape[1] * o.shape[2], -1)

def ctx_attn(q, k, v, sink=None):
    Hq, dq = q.shape[2:]
    Hkv = k.shape[2]
    qg = q.reshape(q.shape[:2] + (Hkv, Hq // Hkv, dq))
    s = jnp.einsum('bqhgd,bkhd->bhgqk', qg, k, preferred_element_type=jnp.float32) * dq ** -0.5
    p = softmax_with_sink(s, sink).astype(v.dtype)
    o = jnp.einsum('bhgqk,bkhd->bqhgd', p, v)
    return o.reshape(o.shape[:2] + (-1,))

def global_attn_blocks(q, k, v):
    Hq, dq = q.shape[2:]
    Hkv = k.shape[2]
    qb = to_blocks(q.reshape(q.shape[:2] + (Hkv, Hq // Hkv, dq)))

    def block(qi):
        s = jnp.einsum('bqhgd,bkhd->bhgqk', qi, k, preferred_element_type=jnp.float32) * dq ** -0.5
        p = jax.nn.softmax(s, axis=-1).astype(v.dtype)
        return jnp.einsum('bhgqk,bkhd->bqhgd', p, v)

    return from_blocks(lax.map(block, qb))

def window_attn_blocks(q, k, v, kc, vc, sink):
    S = q.shape[1]
    Hq, dq = q.shape[2:]
    Hkv = k.shape[2]
    L = kc.shape[1]
    span = Q_BLOCK + 2 * WINDOW
    pad = ((0, 0), (WINDOW, WINDOW), (0, 0), (0, 0))
    kp, vp = jnp.pad(k, pad), jnp.pad(v, pad)
    qb = to_blocks(q.reshape(q.shape[:2] + (Hkv, Hq // Hkv, dq)))
    scale = dq ** -0.5

    def block(args):
        i, qi = args
        kb = lax.dynamic_slice_in_dim(kp, i * Q_BLOCK, span, axis=1)
        vb = lax.dynamic_slice_in_dim(vp, i * Q_BLOCK, span, axis=1)
        qpos = i * Q_BLOCK + jnp.arange(Q_BLOCK)
        kpos = i * Q_BLOCK - WINDOW + jnp.arange(span)
        valid = (jnp.abs(qpos[:, None] - kpos[None, :]) <= WINDOW) & (kpos >= 0)[None, :] & (kpos < S)[None, :]
        s_lat = jnp.einsum('bqhgd,bkhd->bhgqk', qi, kb, preferred_element_type=jnp.float32) * scale
        s_lat = jnp.where(valid, s_lat, -jnp.inf)
        s_ctx = jnp.einsum('bqhgd,bkhd->bhgqk', qi, kc, preferred_element_type=jnp.float32) * scale
        p = softmax_with_sink(jnp.concatenate([s_ctx, s_lat], axis=-1), sink).astype(v.dtype)
        return (jnp.einsum('bhgqk,bkhd->bqhgd', p[..., :L], vc)
                + jnp.einsum('bhgqk,bkhd->bqhgd', p[..., L:], vb))

    return from_blocks(lax.map(block, (jnp.arange(S // Q_BLOCK), qb)))

def neighbourhood_attn_blocks(q, k, v, kc, vc, rpb):
    S = q.shape[1]
    dq = q.shape[3]
    L = kc.shape[1]
    rows = S // GRID_W
    kh = min(NA_KH, rows)
    q_rows = Q_BLOCK // GRID_W
    strip_rows = min(kh + q_rows - 1, rows)
    strip = strip_rows * GRID_W
    qb = to_blocks(q)
    scale = dq ** -0.5
    q_local = jnp.arange(Q_BLOCK)
    k_local = jnp.arange(strip)

    def block(args):
        i, qi = args
        r0 = i * q_rows
        strip_start = jnp.minimum(jnp.clip(r0 - kh // 2, 0, rows - kh), rows - strip_rows)
        kb = lax.dynamic_slice_in_dim(k, strip_start * GRID_W, strip, axis=1)
        vb = lax.dynamic_slice_in_dim(v, strip_start * GRID_W, strip, axis=1)
        qr, qcol = r0 + q_local // GRID_W, q_local % GRID_W
        kr, kcol = strip_start + k_local // GRID_W, k_local % GRID_W
        rs = jnp.clip(qr - kh // 2, 0, rows - kh)
        cs = jnp.clip(qcol - NA_KW // 2, 0, GRID_W - NA_KW)
        valid = ((kr[None, :] >= rs[:, None]) & (kr[None, :] < rs[:, None] + kh)
                 & (kcol[None, :] >= cs[:, None]) & (kcol[None, :] < cs[:, None] + NA_KW))
        dr = jnp.clip(kr[None, :] - qr[:, None] + NA_KH - 1, 0, 2 * NA_KH - 2)
        dc = jnp.clip(kcol[None, :] - qcol[:, None] + NA_KW - 1, 0, 2 * NA_KW - 2)
        bias = rpb[:, dr, dc].astype(jnp.float32)
        s_lat = jnp.einsum('bqhd,bkhd->bhqk', qi, kb, preferred_element_type=jnp.float32) * scale + bias[None]
        s_lat = jnp.where(valid, s_lat, -jnp.inf)
        s_ctx = jnp.einsum('bqhd,bkhd->bhqk', qi, kc, preferred_element_type=jnp.float32) * scale
        p = jax.nn.softmax(jnp.concatenate([s_ctx, s_lat], axis=-1), axis=-1).astype(v.dtype)
        return (jnp.einsum('bhqk,bkhd->bqhd', p[..., :L], vc)
                + jnp.einsum('bhqk,bkhd->bqhd', p[..., L:], vb))

    return from_blocks(lax.map(block, (jnp.arange(S // Q_BLOCK), qb)))

def mixer_a(p, pc, q_g, k_g, cos, sin, with_ctx):
    q, k, v, g = p
    qc, kc, vc, gc = pc
    q = apply_rope(rms_norm(heads(q, A_HEADS), q_g), cos, sin)
    k = apply_rope(rms_norm(heads(k, A_KV_HEADS), k_g), cos, sin)
    kc = rms_norm(heads(kc, A_KV_HEADS), k_g)
    v, vc = heads(v, A_KV_HEADS), heads(vc, A_KV_HEADS)
    o = global_attn_blocks(q, jnp.concatenate([kc, k], axis=1), jnp.concatenate([vc, v], axis=1)) * jax.nn.silu(g)
    if not with_ctx:
        return o, None
    oc = ctx_attn(rms_norm(heads(qc, A_HEADS), q_g), kc, vc) * jax.nn.silu(gc)
    return o, oc

def mixer_b(p, pc, q_g, k_g, rpb, with_ctx):
    q, k, v, g = p
    qc, kc, vc, gc = pc
    q = rms_norm(heads(q, B_HEADS), q_g)
    k = rms_norm(heads(k, B_HEADS), k_g)
    kc = rms_norm(heads(kc, B_HEADS), k_g)
    v, vc = heads(v, B_HEADS), heads(vc, B_HEADS)
    o = neighbourhood_attn_blocks(q, k, v, kc, vc, rpb) * jax.nn.silu(g)
    if not with_ctx:
        return o, None
    oc = ctx_attn(rms_norm(heads(qc, B_HEADS), q_g), kc, vc) * jax.nn.silu(gc)
    return o, oc

def mixer_c(p, pc, q_g, k_g, sink, cos, sin, with_ctx):
    q, k, v, g = p
    qc, kc, vc, gc = pc
    q = apply_rope(rms_norm(heads(q, C_HEADS), q_g), cos, sin)
    k = apply_rope(rms_norm(heads(k, C_KV_HEADS), k_g), cos, sin)
    kc = rms_norm(heads(kc, C_KV_HEADS), k_g)
    v, vc = heads(v, C_KV_HEADS), heads(vc, C_KV_HEADS)
    o = window_attn_blocks(q, k, v, kc, vc, sink) * jax.nn.silu(g)
    if not with_ctx:
        return o, None
    oc = ctx_attn(rms_norm(heads(qc, C_HEADS), q_g), kc, vc, sink) * jax.nn.silu(gc)
    return o, oc

def mixer_d(p, pc, q_g, k_g, kv_g, w_uk, w_uv, cos, sin, with_ctx):
    def keys_values(ckv, k_rope):
        ckv = rms_norm(ckv, kv_g)
        k_nope = heads(ckv @ w_uk, D_HEADS)
        v = heads(ckv @ w_uv, D_HEADS)
        k_rope = jnp.broadcast_to(k_rope[:, :, None, :], k_nope.shape[:-1] + (MLA_ROPE,))
        return rms_norm(jnp.concatenate([k_nope, k_rope], axis=-1), k_g), v

    def rope_tail(t):
        return jnp.concatenate([t[..., :MLA_NOPE], apply_rope(t[..., MLA_NOPE:], cos, sin)], axis=-1)

    q, ckv, k_rope, g = p
    qc, ckv_c, k_rope_c, gc = pc
    q = rope_tail(rms_norm(heads(q, D_HEADS), q_g))
    k, v = keys_values(ckv, k_rope)
    k = rope_tail(k)
    kc, vc = keys_values(ckv_c, k_rope_c)
    o = global_attn_blocks(q, jnp.concatenate([kc, k], axis=1), jnp.concatenate([vc, v], axis=1)) * jax.nn.silu(g)
    if not with_ctx:
        return o, None
    oc = ctx_attn(rms_norm(heads(qc, D_HEADS), q_g), kc, vc) * jax.nn.silu(gc)
    return o, oc

def first_inputs(seed: int = 0) -> dict:
    key = jax.random.key(seed)
    ks = jax.random.split(key, 22)
    f32 = jnp.float32

    def normal(k, shape, scale=1.0):
        return scale * jax.random.normal(k, shape, f32)

    def gain(k, shape):
        return 1.0 + 0.05 * jax.random.normal(k, shape, f32)

    D = D_MODEL
    return {
        'x': normal(ks[0], (BATCH, SEQ, D)),
        'c': normal(ks[1], (BATCH, D)),
        'ctx': normal(ks[2], (BATCH, CTX_LEN, D)),
        'c_ctx': normal(ks[3], (D,)),
        'norm_g': gain(ks[4], (DEPTH, D)),
        'w_ada': normal(ks[5], (DEPTH, D, 3 * D), 0.5 * D ** -0.5),
        'b_ada': normal(ks[6], (DEPTH, 3 * D), 0.01),
        'w_in': normal(ks[7], (DEPTH, D, IN_COLS), D ** -0.5),
        'w_out': normal(ks[8], (DEPTH, MIX_W, D), MIX_W ** -0.5),
        'a_q_g': gain(ks[9], (DEPTH, HEAD_DIM)),
        'a_k_g': gain(ks[10], (DEPTH, HEAD_DIM)),
        'b_q_g': gain(ks[11], (DEPTH, HEAD_DIM)),
        'b_k_g': gain(ks[12], (DEPTH, HEAD_DIM)),
        'b_rpb': normal(ks[13], (DEPTH, B_HEADS, 2 * NA_KH - 1, 2 * NA_KW - 1), 0.1),
        'c_q_g': gain(ks[14], (DEPTH, HEAD_DIM)),
        'c_k_g': gain(ks[15], (DEPTH, HEAD_DIM)),
        'c_sink': normal(ks[16], (DEPTH, C_HEADS), 0.5),
        'd_q_g': gain(ks[17], (DEPTH, MLA_QK)),
        'd_k_g': gain(ks[18], (DEPTH, MLA_QK)),
        'd_kv_g': gain(ks[19], (DEPTH, MLA_KV_RANK)),
        'd_w_uk': normal(ks[20], (DEPTH, MLA_KV_RANK, D_HEADS * MLA_NOPE), MLA_KV_RANK ** -0.5),
        'd_w_uv': normal(ks[21], (DEPTH, MLA_KV_RANK, D_HEADS * MLA_V), MLA_KV_RANK ** -0.5),
    }

def first_block(x, c, ctx, c_ctx, norm_g, w_ada, b_ada, w_in, w_out,
              a_q_g, a_k_g, b_q_g, b_k_g, b_rpb, c_q_g, c_k_g, c_sink,
              d_q_g, d_k_g, d_kv_g, d_w_uk, d_w_uv):
    S = x.shape[1]
    cos_h, sin_h = axial_rope_tables(S, HEAD_DIM)
    cos_r, sin_r = axial_rope_tables(S, MLA_ROPE)
    hc = ctx.astype(x.dtype)
    for l in range(DEPTH):
        with_ctx = l < DEPTH - 1
        sh_x, sc_x, gt_x = jnp.split((jax.nn.silu(c) @ w_ada[l] + b_ada[l])[:, None, :], 3, axis=-1)
        sh_c, sc_c, gt_c = jnp.split(jax.nn.silu(c_ctx) @ w_ada[l] + b_ada[l], 3, axis=-1)
        h_x = rms_norm(x, norm_g[l]) * (1 + sc_x) + sh_x
        h_c = rms_norm(hc, norm_g[l]) * (1 + sc_c) + sh_c
        px = split_cols(h_x @ w_in[l])
        pc = split_cols(h_c @ w_in[l])
        oa, oa_c = mixer_a(px[0:4], pc[0:4], a_q_g[l], a_k_g[l], cos_h, sin_h, with_ctx)
        ob, ob_c = mixer_b(px[4:8], pc[4:8], b_q_g[l], b_k_g[l], b_rpb[l], with_ctx)
        oc, oc_c = mixer_c(px[8:12], pc[8:12], c_q_g[l], c_k_g[l], c_sink[l], cos_h, sin_h, with_ctx)
        od, od_c = mixer_d(px[12:16], pc[12:16], d_q_g[l], d_k_g[l], d_kv_g[l], d_w_uk[l], d_w_uv[l],
                           cos_r, sin_r, with_ctx)
        x = x + gt_x * (jnp.concatenate([oa, ob, oc, od], axis=-1) @ w_out[l])
        if with_ctx:
            hc = hc + gt_c * (jnp.concatenate([oa_c, ob_c, oc_c, od_c], axis=-1) @ w_out[l])
    return x


DEPTH_2 = 2


POOL_WINDOWS = (2, 4, 8, 16)
POOL_GROUPS = len(POOL_WINDOWS)
POOL_WIDTH = D_MODEL // 2
POOL_GC = POOL_WIDTH // POOL_GROUPS

DSA_HEADS = 16
DSA_HEAD_DIM = 64
DSA_WIDTH = DSA_HEADS * DSA_HEAD_DIM
IDX_HEADS = 16
IDX_DIM = 64
DSA_MAX_TOPK = 256

SWA_Q_HEADS = 32
SWA_KV_HEADS = 4
SWA_HEAD_DIM = 64
SWA_WIDTH = SWA_Q_HEADS * SWA_HEAD_DIM

NUM_BUCKETS = 32
MAX_DISTANCE = 1024
BIAS_HEADS = 32

EVEN_SPLITS = (POOL_WIDTH, POOL_WIDTH,
               DSA_WIDTH, DSA_HEAD_DIM, DSA_HEAD_DIM,
               DSA_WIDTH,
               IDX_HEADS * IDX_DIM, IDX_DIM, IDX_HEADS)
EVEN_IN = sum(EVEN_SPLITS)
EVEN_OUT_IN = POOL_WIDTH + DSA_WIDTH
ODD_SPLITS = (SWA_WIDTH, SWA_KV_HEADS * SWA_HEAD_DIM, SWA_KV_HEADS * SWA_HEAD_DIM, SWA_WIDTH)
ODD_IN = sum(ODD_SPLITS)


def rms_norm_2(x, g):
    xf = x.astype(jnp.float32)
    y = xf * lax.rsqrt(jnp.mean(xf * xf, axis=-1, keepdims=True) + EPS) * g.astype(jnp.float32)
    return y.astype(x.dtype)

def split_cols_2(h, sizes):
    return jnp.split(h, np.cumsum(sizes)[:-1].tolist(), axis=-1)

def t5_bucket(n):
    n = jnp.maximum(n, 0)
    max_exact = NUM_BUCKETS // 2
    nf = jnp.maximum(n, 1).astype(jnp.float32)
    large = max_exact + (jnp.log(nf / max_exact) / math.log(MAX_DISTANCE / max_exact)
                         * (NUM_BUCKETS - max_exact)).astype(jnp.int32)
    large = jnp.minimum(large, NUM_BUCKETS - 1)
    return jnp.where(n < max_exact, n, large)

def causal_multiscale_pool(a):
    B, T, G, C = a.shape
    cs = jnp.cumsum(a.astype(jnp.float32), axis=1)
    csp = jnp.concatenate([jnp.zeros((B, 1, G, C), jnp.float32), cs], axis=1)
    t = jnp.arange(T)
    outs = []
    for g, w in enumerate(POOL_WINDOWS):
        lo = jnp.maximum(t + 1 - w, 0)
        s = csp[:, t + 1, g] - csp[:, lo, g]
        cnt = (t + 1 - lo).astype(jnp.float32)
        outs.append(s / cnt[None, :, None])
    return jnp.stack(outs, axis=2).astype(a.dtype)

def dsa_attention(q, k, v, iq, ik, iw, rel_bias, topk):
    B, T, H, d = q.shape
    nb = T // Q_BLOCK
    scale = DSA_HEAD_DIM ** -0.5
    keys = jnp.arange(T)

    def to_blocks(z):
        return jnp.swapaxes(z.reshape((B, nb, Q_BLOCK) + z.shape[2:]), 0, 1)

    def block_fn(args):
        qb, iqb, iwb, start = args
        pos_q = start + jnp.arange(Q_BLOCK)
        s_idx = jnp.einsum('bqhe,bse->bqhs', iqb, ik).astype(jnp.float32) * (IDX_DIM ** -0.5)
        score = jnp.einsum('bqhs,bqh->bqs', jax.nn.relu(s_idx), iwb.astype(jnp.float32))
        score = jnp.where(keys[None, None, :] <= pos_q[None, :, None], score, -jnp.inf)
        _, idx = lax.top_k(score, topk)
        valid = idx <= pos_q[None, :, None]
        kg = jax.vmap(lambda kk, ii: kk[ii])(k, idx)
        vg = jax.vmap(lambda vv, ii: vv[ii])(v, idx)
        logits = jnp.einsum('bqhd,bqkd->bhqk', qb, kg).astype(jnp.float32) * scale
        bias = rel_bias[t5_bucket(pos_q[None, :, None] - idx)][..., :H]
        logits = logits + jnp.transpose(bias, (0, 3, 1, 2)).astype(jnp.float32)
        logits = jnp.where(valid[:, None], logits, -jnp.inf)
        p = jax.nn.softmax(logits, axis=-1).astype(vg.dtype)
        return jnp.einsum('bhqk,bqkd->bqhd', p, vg)

    starts = jnp.arange(nb) * Q_BLOCK
    out = lax.map(block_fn, (to_blocks(q), to_blocks(iq), to_blocks(iw), starts))
    return jnp.swapaxes(out, 0, 1).reshape(B, T, H, d)

def swa_sink_attention(q, k, v, sinks, rel_bias):
    B, T, HQ, d = q.shape
    HKV = k.shape[2]
    G = HQ // HKV
    W = WINDOW
    nb = T // W
    qb = q.reshape(B, nb, W, HKV, G, d)

    def with_prev(z):
        zb = z.reshape(B, nb, W, HKV, d)
        prev = jnp.concatenate([jnp.zeros_like(zb[:, :1]), zb[:, :-1]], axis=1)
        return jnp.concatenate([prev, zb], axis=2)

    kw, vw = with_prev(k), with_prev(v)
    logits = jnp.einsum('bnqhgd,bnkhd->bnhgqk', qb, kw).astype(jnp.float32) * (d ** -0.5)
    i = jnp.arange(W)
    j = jnp.arange(2 * W)
    dist = W + i[:, None] - j[None, :]
    bias = rel_bias[t5_bucket(dist)][..., :HQ]
    bias = jnp.transpose(bias, (2, 0, 1)).reshape(HKV, G, W, 2 * W).astype(jnp.float32)
    in_window = (dist >= 0) & (dist < W)
    has_prev = (jnp.arange(nb)[:, None, None] > 0) | (j[None, None, :] >= W)
    mask = in_window[None] & has_prev
    logits = jnp.where(mask[None, :, None, None], logits + bias, -jnp.inf)
    sink = jnp.broadcast_to(sinks.astype(jnp.float32).reshape(HKV, G)[None, None, :, :, None, None],
                            (B, nb, HKV, G, W, 1))
    p = jax.nn.softmax(jnp.concatenate([logits, sink], axis=-1), axis=-1)[..., :-1]
    out = jnp.einsum('bnhgqk,bnkhd->bnqhgd', p.astype(vw.dtype), vw)
    return out.reshape(B, T, HQ * d)

def even_layer(x, norm_g, w_in, pool_w, pool_scale, q_gain, k_gain, w_out, rel_bias):
    B, T, _ = x.shape
    h = rms_norm_2(x, norm_g) @ w_in
    p_in, p_gate, dq, dk, dv, d_gate, iq, ik, iw = split_cols_2(h, EVEN_SPLITS)
    pa = p_in.reshape(B, T, POOL_GROUPS, POOL_GC)
    pooled = causal_multiscale_pool(pa) - pa
    py = jnp.einsum('btgc,gcd->btgd', pooled, pool_w) * pool_scale.reshape(POOL_GROUPS, POOL_GC)
    py = jax.nn.silu(p_gate) * py.reshape(B, T, POOL_WIDTH)
    q = rms_norm_2(dq.reshape(B, T, DSA_HEADS, DSA_HEAD_DIM), q_gain)
    k = rms_norm_2(dk, k_gain)
    iq = iq.reshape(B, T, IDX_HEADS, IDX_DIM)
    iw = iw * (IDX_HEADS ** -0.5)
    topk = min(DSA_MAX_TOPK, T // 4)
    o = dsa_attention(q, k, dv, iq, ik, iw, rel_bias, topk)
    dy = jax.nn.silu(d_gate) * o.reshape(B, T, DSA_WIDTH)
    return x + jnp.concatenate([py, dy], axis=-1) @ w_out

def odd_layer(x, norm_g, w_in, q_gain, k_gain, sinks, w_out, rel_bias):
    B, T, _ = x.shape
    h = rms_norm_2(x, norm_g) @ w_in
    q, k, v, gate = split_cols_2(h, ODD_SPLITS)
    q = rms_norm_2(q.reshape(B, T, SWA_Q_HEADS, SWA_HEAD_DIM), q_gain)
    k = rms_norm_2(k.reshape(B, T, SWA_KV_HEADS, SWA_HEAD_DIM), k_gain)
    v = v.reshape(B, T, SWA_KV_HEADS, SWA_HEAD_DIM)
    o = swa_sink_attention(q, k, v, sinks, rel_bias)
    return x + (jax.nn.silu(gate) * o) @ w_out

def second_inputs(seed: int = 0) -> dict:
    key = jax.random.key(seed)
    ks = jax.random.split(key, 16)
    n_even = (DEPTH_2 + 1) // 2
    n_odd = DEPTH_2 // 2
    nrm = jax.random.normal
    f32 = jnp.float32
    return {
        "x": nrm(ks[0], (BATCH, SEQ, D_MODEL), f32),
        "rel_bias": 0.5 * nrm(ks[1], (NUM_BUCKETS, BIAS_HEADS), f32),
        "even_norm": 1.0 + 0.02 * nrm(ks[2], (n_even, D_MODEL), f32),
        "even_w_in": nrm(ks[3], (n_even, D_MODEL, EVEN_IN), f32) * D_MODEL ** -0.5,
        "even_pool_w": nrm(ks[4], (n_even, POOL_GROUPS, POOL_GC, POOL_GC), f32) * POOL_GC ** -0.5,
        "even_pool_scale": 1.0 + 0.02 * nrm(ks[5], (n_even, POOL_WIDTH), f32),
        "even_q_gain": 1.0 + 0.02 * nrm(ks[6], (n_even, DSA_HEAD_DIM), f32),
        "even_k_gain": 1.0 + 0.02 * nrm(ks[7], (n_even, DSA_HEAD_DIM), f32),
        "even_w_out": nrm(ks[8], (n_even, EVEN_OUT_IN, D_MODEL), f32) * EVEN_OUT_IN ** -0.5,
        "odd_norm": 1.0 + 0.02 * nrm(ks[9], (n_odd, D_MODEL), f32),
        "odd_w_in": nrm(ks[10], (n_odd, D_MODEL, ODD_IN), f32) * D_MODEL ** -0.5,
        "odd_q_gain": 1.0 + 0.02 * nrm(ks[11], (n_odd, SWA_HEAD_DIM), f32),
        "odd_k_gain": 1.0 + 0.02 * nrm(ks[12], (n_odd, SWA_HEAD_DIM), f32),
        "odd_sinks": nrm(ks[13], (n_odd, SWA_Q_HEADS), f32),
        "odd_w_out": nrm(ks[14], (n_odd, SWA_WIDTH, D_MODEL), f32) * SWA_WIDTH ** -0.5,
    }

def second_block(x, rel_bias, even_norm, even_w_in, even_pool_w, even_pool_scale, even_q_gain,
              even_k_gain, even_w_out, odd_norm, odd_w_in, odd_q_gain, odd_k_gain, odd_sinks,
              odd_w_out):
    for layer in range(DEPTH_2):
        i = layer // 2
        if layer % 2 == 0:
            x = even_layer(x, even_norm[i], even_w_in[i], even_pool_w[i], even_pool_scale[i],
                           even_q_gain[i], even_k_gain[i], even_w_out[i], rel_bias)
        else:
            x = odd_layer(x, odd_norm[i], odd_w_in[i], odd_q_gain[i], odd_k_gain[i],
                          odd_sinks[i], odd_w_out[i], rel_bias)
    return x


def setup_inputs(seed=0):
    out = dict(first_inputs(seed))
    for name, value in second_inputs(seed + 1).items():
        if name != "x":
            out[name + "_2"] = value
    return out


def reference(
    x, c, ctx, c_ctx, norm_g, w_ada, b_ada, w_in, w_out, a_q_g, a_k_g, b_q_g, b_k_g, b_rpb,
    c_q_g, c_k_g, c_sink, d_q_g, d_k_g, d_kv_g, d_w_uk, d_w_uv, rel_bias_2, even_norm_2,
    even_w_in_2, even_pool_w_2, even_pool_scale_2, even_q_gain_2, even_k_gain_2, even_w_out_2,
    odd_norm_2, odd_w_in_2, odd_q_gain_2, odd_k_gain_2, odd_sinks_2, odd_w_out_2,
):
    x = first_block(
        x, c, ctx, c_ctx, norm_g, w_ada, b_ada, w_in, w_out, a_q_g, a_k_g, b_q_g, b_k_g, b_rpb,
        c_q_g, c_k_g, c_sink, d_q_g, d_k_g, d_kv_g, d_w_uk, d_w_uv,
    )
    return second_block(
        x, rel_bias_2, even_norm_2, even_w_in_2, even_pool_w_2, even_pool_scale_2,
        even_q_gain_2, even_k_gain_2, even_w_out_2, odd_norm_2, odd_w_in_2, odd_q_gain_2,
        odd_k_gain_2, odd_sinks_2, odd_w_out_2,
    )


_drawn_inputs = setup_inputs


def setup_inputs(seed=0):
    import zlib

    import numpy as np

    out = dict(_drawn_inputs(seed))
    spreads = {}
    factors = {'ctx': 4.438,
     'norm_g': 8.0,
     'b_ada': 8.0,
     'a_q_g': 8.0,
     'a_k_g': 8.0,
     'b_q_g': 8.0,
     'b_k_g': 8.0,
     'b_rpb': 8.0,
     'c_q_g': 8.0,
     'c_k_g': 8.0,
     'c_sink': 8.0,
     'd_q_g': 8.0,
     'd_k_g': 8.0,
     'd_kv_g': 8.0,
     'd_w_uk': 7.342,
     'even_norm_2': 4.371,
     'even_pool_scale_2': 8.0,
     'even_q_gain_2': 8.0,
     'even_k_gain_2': 8.0,
     'odd_norm_2': 8.0,
     'odd_q_gain_2': 8.0,
     'odd_k_gain_2': 8.0,
     'odd_sinks_2': 50.979}
    for name, (base, spread) in spreads.items():
        noise = np.random.default_rng([zlib.crc32(name.encode()), seed]).standard_normal(out[name].shape)
        drawn = base * np.exp(spread * noise) if base else spread * noise
        out[name] = jnp.asarray(drawn.astype(out[name].dtype))
    for name, factor in factors.items():
        out[name] = (out[name] * factor).astype(out[name].dtype)
    return out
```

```python
from contextlib import ExitStack

import numpy as np

import concourse.bass as bass
from concourse import mybir

F32 = mybir.dt.float32
F32R = mybir.dt.float32r
ALU = mybir.AluOpType
ACT = mybir.ActivationFunctionType
AX = mybir.AxisListType.X

P = 128
D = 2048
KT = D // P
HALF = KT // 2
SEQ, CTX = 512, 256
TOK = SEQ + CTX
QT = SEQ // P
EPS = 1e-6
NEG = -1e30
GRID_W = 64
HEAD = 128
NOPE, ROPE = 128, 64
RANK = 512
NBUCKET, BIAS_HEADS = 32, 32
ADA_CALLS = 3 * KT
SHIFT, SCALE, GATE_COL = 0, KT, 2 * KT
POOL_WINDOWS = (2, 4, 8, 16)
TOPK = 128
DSA_HEADS = 16
NDIST = 640
NDIST_W = 384
RPB_H, RPB_W = 15, 31
RPB_FLAT = 4 * RPB_H * RPB_W + 2 * GRID_W

A0, B0, C0, D0 = 0, 1536, 3584, 5120
E_PIN, E_PGATE, E_Q, E_KV, E_DGATE, E_IQ, E_IK, E_IW = 0, 1024, 2048, 3072, 3200, 4224, 5248, 5312
O_Q, O_K, O_V, O_GATE = 0, 2048, 2304, 2560

COL_LIST = (("norm_g", 16), ("b_ada", 48), ("cond", 32), ("even_norm", 16), ("odd_norm", 16),
            ("pool_scale", 8), ("a_q", 1), ("a_k", 1), ("b_q", 1), ("b_k", 1), ("c_q", 1), ("c_k", 1),
            ("d_kv", 4), ("d_qn", 1), ("d_qr", 1), ("d_kn", 1), ("d_kr", 1), ("e_q", 1), ("e_k", 1),
            ("o_q", 1), ("o_k", 1), ("c_sink", 4), ("o_sink", 32))
COL = {}
_at = 0
for _n, _w in COL_LIST:
    COL[_n] = _at
    _at += _w
NCOL = _at


def shape_constants():
    t = {}
    t["ident"] = np.eye(P, dtype=np.float32)
    t["ones"] = np.ones((P, P), np.float32)
    half = np.arange(P) // 64
    t["ones64"] = (half[:, None] == half[None, :]).astype(np.float32)
    for name, rot in (("swap_a", HEAD), ("swap_d", ROPE)):
        partner = (np.arange(P) // rot) * rot + (np.arange(P) % rot + rot // 2) % rot
        t[name] = (np.arange(P)[:, None] == partner[None, :]).astype(np.float32)
    tok = np.arange(SEQ)
    row, col = (tok // GRID_W).astype(np.float32), (tok % GRID_W).astype(np.float32)
    for name, rot in (("rope_a", HEAD), ("rope_d", ROPE)):
        n = rot // 4
        inv = (np.float32(10000.0) ** (-np.arange(n, dtype=np.float32) / np.float32(n))).astype(np.float32)
        ang = np.concatenate([row[:, None] * inv, col[:, None] * inv], axis=-1).astype(np.float32).T
        cos, sin = np.cos(ang).astype(np.float32), np.sin(ang).astype(np.float32)
        reps = P // rot
        t[name] = np.concatenate([np.tile(np.concatenate([cos, cos]), (reps, 1)),
                                  np.tile(np.concatenate([-sin, sin]), (reps, 1))], axis=1)
    m = np.arange(NDIST)
    dist = SEQ - 1 - m
    bucket = np.zeros(NDIST, np.int64)
    for i, n in enumerate(dist):
        n = int(max(n, 0))
        if n < NBUCKET // 2:
            bucket[i] = n
        else:
            k = 0
            while k + 1 < 16 and n ** 16 >= (16 ** 16) * 64 ** (k + 1):
                k += 1
            bucket[i] = 16 + k
    t["onehot"] = (np.arange(NBUCKET)[:, None] == bucket[None, :]).astype(np.float32)
    causal = np.where(dist >= 0, 0.0, NEG)
    window = np.where((dist >= 0) & (dist < P), 0.0, NEG)[NDIST - NDIST_W:]
    t["dist_mask"] = np.tile(np.concatenate([causal, window])[None], (BIAS_HEADS, 1)).astype(np.float32)
    p, j = np.arange(P)[:, None], np.arange(3 * P)[None, :]
    win = np.where(np.abs(p + P - j) <= P, 0.0, NEG)
    qc, kc = (np.arange(P) % GRID_W)[:, None], np.arange(GRID_W)[None, :]
    cs = np.clip(qc - 8, 0, GRID_W - 16)
    colm = np.where((kc >= cs) & (kc < cs + 16), 0.0, NEG)
    inv = np.stack([1.0 / np.minimum(np.arange(16) + 1, w) for w in POOL_WINDOWS])
    t["masks"] = np.concatenate([win, np.zeros((P, CTX)), colm], axis=1).astype(np.float32)
    t["tri"] = np.where(np.arange(P)[None, :] <= np.arange(P)[:, None], 0.0, NEG).astype(np.float32)
    t["inv_count"] = np.tile(inv.reshape(1, -1), (P, 1)).astype(np.float32)
    return t


class Group:

    def __init__(self, kind, n=SEQ, gain=None, rotate=False, ones="ones", per=HEAD, dst=None, j=0, width=P,
                 layer=0):
        self.kind, self.n, self.gain, self.rotate, self.ones, self.per = kind, n, gain, rotate, ones, per
        self.dst, self.j, self.width, self.layer = dst, j, width, layer
        self.gate_cols, self.gate_after, self.fill, self.weights = (), 0, None, None
        self.src, self.dmas, self.raw_free, self.landed, self.rs, self.cs, self.split = None, 0, None, 0, 0, 0, True
        self.g = self.r = self.c = self.norm = self.stage = self.aux = self.rope = self.silu = 0
        self.copy = self.resid = self.fp32 = 0
        self.phase, self.next, self.primed, self.saves, self.whole = 1, None, False, False, False

    def at(self, shift, dma):
        new = Group(self.kind, self.n, self.gain, self.rotate, self.ones, self.per, self.dst, self.j, self.width,
                    self.layer)
        new.js, new.split, new.dmas, new.rs, new.cs, new.phase, new.primed = (
            self.js, self.split, self.dmas, self.rs, self.cs, self.phase, self.primed)
        new.j, new.g, new.r, new.c = self.j + shift, self.g + shift, self.r + shift, self.c + shift
        new.norm, new.stage, new.aux = self.norm + shift, self.stage + shift, self.aux + shift
        new.rope, new.silu, new.copy = self.rope + shift, self.silu + shift, self.copy + shift
        new.resid, new.landed = self.resid + shift, self.landed + dma
        new.acc_free = (self.acc_free[0], self.acc_free[1] + shift)
        new.raw_free = (self.raw_free[0], self.raw_free[1] + shift * self.raw_free[2], self.raw_free[2])
        new.src = (self.src[0], self.src[1] + P * shift)
        return new


def spans(n):
    return [(0, min(n, 512))] + ([(512, n)] if n > 512 else [])


def keys(mixer, qt):
    return TOK if mixer != "c" else CTX + P * (3 if 0 < qt < QT - 1 else 2)


class Links:

    def __init__(self, eng, sem):
        self.eng, self.sem, self.n, self.more = eng, sem, 0, 0

    def done(self, ins):
        ins.then_inc(self.sem, 1)
        self.n += 1

    def wait(self):
        self.eng.wait_ge(self.sem, self.n + self.more)

    def link(self, ins):
        self.done(ins)
        self.wait()

    def enter(self, i, per):
        self.start, self.per, self.more = self.n, per, i * per

    def leave(self, times):
        assert self.n - self.start == self.per, (self.n - self.start, self.per)
        self.n, self.more = self.start + self.per * times, 0


def plan():
    count = dict(g=0, r=0, c=0, norm=0, stage=0, aux=0, rope=0, silu=0, copy=0, resid=0, fp32=0)
    landed = [0, 0]
    raw_free, acc_free = [], []
    order = []

    def group(kind, w, col, **kw):
        G = Group(kind, **kw)
        G.js = G.j % 2
        G.split = kind not in ("kn", "vn")
        G.src = (w, col) if w else None
        if G.split:
            G.g = count["g"]
            count["g"] += 1
        if w:
            G.r, G.rs = count["r"], count["r"] % 2
            count["r"] += 1
            G.raw_free = raw_free[G.r - 2] if G.r >= 2 else None
            G.dmas = {"qr": 2, "kr": 2, "ikw": 3}.get(kind, 1)
            landed[G.rs] += 16 * G.dmas
            G.landed = landed[G.rs]
            raw_free.append(("lo_done", 2 * G.g + 2, 2) if G.split else None)
        G.c, G.cs = count["c"], count["c"] % 2
        count["c"] += 1
        G.acc_free = acc_free[G.c - 2] if G.c >= 2 else None
        if kind in ("norm", "qn", "kn", "kvn", "ckv"):
            G.norm = count["norm"]
            if kind != "ckv" or G.j == 3:
                count["norm"] += 1
        if kind in ("norm", "qn", "kn", "kvn", "ckv", "plain", "ikw"):
            G.stage = count["stage"]
            count["stage"] += 1
        if kind in ("plain", "ikw", "kvn"):
            G.aux = count["aux"]
            count["aux"] += 1
        if G.rotate:
            G.aux = count["aux"]
            count["aux"] += 1
            G.rope = count["rope"]
            count["rope"] += 1
        if kind == "pin" and G.j % 2:
            G.aux = count["aux"]
            count["aux"] += 2
        if kind == "final":
            G.aux = count["aux"]
            count["aux"] += 1
        if kind == "silu":
            G.silu = count["silu"]
            G.saves = G.dst == "OT" and G.j == 8
            count["silu"] += 1
        if kind in ("copy", "qr", "kr", "pin", "vn"):
            G.copy = count["copy"]
            count["copy"] += 1
        if kind in ("kn", "vn"):
            G.fp32 = count["fp32"]
            count["fp32"] += 1
        if kind in ("wout", "final"):
            G.resid = count["resid"]
            count["resid"] += 1
        acc_free.append({"norm": ("xn_done", G.norm + 1),
                         "qn": ("xn_done", G.norm + 1),
                         "kn": ("xn_done", G.norm + 1),
                         "kvn": ("xn_done", G.norm + 1),
                         "ckv": ("staged", G.stage + 1),
                         "plain": ("staged", G.stage + 1),
                         "ikw": ("staged", G.stage + 1),
                         "silu": ("silu_done", G.silu + 1),
                         "wout": ("resid_done", G.resid + 1),
                         "final": ("resid_done", G.resid + 1)}.get(
                             kind, ("copied", G.copy + 1)))
        return G

    def run(groups, **kw):
        groups[0].fill = kw.pop("fill", None)
        order.append(("run", dict(groups=groups, **kw)))

    def stage(name, **kw):
        order.append((name, dict(kw, total=dict(count))))

    def mixer(m, c0, heads_kv, rotate):
        q, k = f"{m}_q", f"{m}_k"
        gs = [group("norm", "w_in", c0 + 512 + P * j, n=TOK, gain=k, rotate=rotate, dst="K", j=j)
              for j in range(heads_kv)]
        gs += [group("plain", "w_in", c0 + 512 + P * (heads_kv + j), n=TOK, j=j, dst="V",
                     width=P * heads_kv) for j in range(heads_kv)]
        gs += [group("norm", "w_in", c0 + P * j, gain=q, rotate=rotate, dst="Q", j=j) for j in range(4)]
        gs += [group("silu", "w_in", c0 + 512 + 2 * P * heads_kv + P * j, j=j, dst="GATE")
               for j in range(4)]
        for s in range(8):
            if m == "a":
                gs[4 + s].gate_cols = (2 * s, 2 * s + 1)
                gs[4 + s].gate_after = gs[3].aux + 1
        return gs

    stage("start")
    for m, c0, kv, rotate in (("a", A0, 2, True), ("b", B0, 4, False), ("c", C0, 2, True)):
        run(mixer(m, c0, kv, rotate), fill=0 if m == "a" else None)
        stage("attend", mixer=m)
    q0, lat = D0, D0 + 768
    gs = [group("qr", "w_in", (q0 + 384 * p + 128, q0 + 384 * p + 320), j=p) for p in range(2)]
    gs2 = [group("qn", "w_in", q0 + 192 * h, gain="d_qn", j=h, dst="Q", rotate=h % 2 == 1) for h in range(4)]
    gs3 = [group("silu", "w_in", lat + 512 + 64 + P * j, j=j, dst="GATE") for j in range(4)]
    gs4 = [group("kr", "w_in", lat + 512, n=TOK, j=0)]
    gs5 = [group("ckv", "w_in", lat + P * j, n=TOK, j=j) for j in range(4)]
    run(gs + gs2 + gs3 + gs4 + gs5)
    stage("latent")
    kn, vn = [], []
    for h in range(TOK // P):
        if h < 4:
            kn.append(group("kn", None if h else "w_uk", 0, n=TOK, gain="d_kn", j=h, dst="K", rotate=h % 2 == 1))
            kn[h].weights = kn[0]
        vn.append(group("vn", None if h else "w_uv", 0, j=h))
        vn[h].weights = vn[0]
    raw_free[kn[0].r] = ("fp32_done", kn[-1].fp32 + 1, 1)
    raw_free[vn[0].r] = ("fp32_done", vn[-1].fp32 + 1, 1)
    run([G for h in range(TOK // P) for G in kn[h:h + 1] + vn[h:h + 1]])
    stage("attend", mixer="d")
    stage("join", fill=1)
    run([group("wout", "w_out", P * j, j=j, layer=0) for j in range(KT)], fill=1, loop=True)
    stage("normalise", layer=1, fill=2)
    run([group("copy", "even_w_in", E_IQ + P * j, j=j, dst="IQ") for j in range(8)], fill=2, loop=True)
    run([group("ikw", "even_w_in", 0, j=0)])
    stage("index")
    run([group("silu", "even_w_in", E_PGATE + P * j, j=j, dst="OT") for j in range(8)], loop=True)
    run([group("norm", "even_w_in", E_Q + P * j, gain="e_q", ones="ones64", per=64, j=j, dst="Q2")
         for j in range(8)], loop=True)
    run([group("kvn", "even_w_in", E_KV, gain="e_k", ones="ones64", per=64, j=0)])
    run([group("pin", "even_w_in", E_PIN + P * j, j=j) for j in range(8)])
    run([group("silu", "even_w_in", E_DGATE + P * j, j=8 + j, dst="OT") for j in range(8)], loop=True)
    stage("dsa")
    stage("join", fill=3)
    run([group("wout", "even_w_out", P * j, j=j, layer=1) for j in range(KT)], fill=3, loop=True)
    stage("normalise", layer=2, fill=4)
    run([group("norm", "odd_w_in", O_K + P * j, gain="o_k", ones="ones64", per=64, j=j, dst="K3")
         for j in range(2)] +
        [group("plain", "odd_w_in", O_V + P * j, j=j, dst="V3", width=256) for j in range(2)], fill=4)
    run([group("norm", "odd_w_in", O_Q + P * j, gain="o_q", ones="ones64", per=64, j=j, dst="Q3")
         for j in range(KT)], loop=True)
    run([group("silu", "odd_w_in", O_GATE + P * j, j=j, dst="OT") for j in range(KT)], loop=True)
    stage("swa")
    stage("join", fill=5)
    run([group("final", "odd_w_out", P * j, j=j, layer=2) for j in range(KT)], fill=5, loop=True)
    stage("end")
    return order


def build(nc, T, out):
    order = plan()
    K1 = 1024
    base = 16512
    top = [0]

    def at(name, cols, off, dt=F32, rows=P):
        top[0] = max(top[0], off + 4 * cols)
        assert off + 4 * cols <= nc.sbuf_usable_end - base, name
        return nc.alloc_sbuf_tensor_at(name, [rows, cols], dt, offset=base + off)

    H1H, H1L = at("h1_hi", KT * TOK, 0, F32R), at("h1_lo", KT * TOK, 48 * K1, F32R)
    H2H, H2L = at("h2_hi", KT * SEQ, 0, F32R), at("h2_lo", KT * SEQ, 32 * K1, F32R)
    OT = at("out_t", KT * SEQ, 64 * K1)
    XNAT = at("x_natural", 6 * D, 0)
    ADAR = at("ada_ring", 4 * KT * P, 48 * K1)
    RAW = [at(f"raw{s}", KT * P, (96 + 8 * s) * K1) for s in range(2)]
    WH = [at(f"w_hi{s}", HALF * P, (112 + 4 * s) * K1, F32R) for s in range(2)]
    WL = [at(f"w_lo{s}", HALF * P, (120 + 4 * s) * K1, F32R) for s in range(2)]
    AROW = at("ada_rows", 4096, 112 * K1, rows=2)
    small, high = [128 * K1], [207 * K1]

    def const(name, cols, area=small):
        t = at(name, cols, area[0])
        area[0] += -(-4 * cols // 32) * 32
        assert small[0] <= 136 * K1
        return t

    IDENT, ONES, ONES64 = const("ident_sb", P), const("ones_sb", P), const("ones64_sb", P)
    SWAP_A, SWAP_D = const("swap_a_sb", P), const("swap_d_sb", P)
    ROPE_T = const("rope_sb", 2 * SEQ)
    COLS = const("cols_sb", NCOL)
    ADA = const("ada_sb", ADA_CALLS * 2)
    CS = const("cond_silu", 2 * KT, high)
    EPS_T = const("eps_sb", 1)
    INVC = const("inv_count_sb", 4 * 16, high)
    MX, NG, SM, RI, ES = (const(n, 8) for n in ("row_max", "neg_max", "row_sum", "row_inv", "sink_exp"))
    M8 = const("top8", 3 * 8, high)
    IW = const("index_weight", QT * 16, high)
    Q, K = at("q_t", 4 * SEQ, 136 * K1), at("k_t", 4 * TOK, 144 * K1)
    V, VA = at("v_nat", 6 * 512, 156 * K1), at("v_nat_ac", 6 * 256, 150 * K1)
    GADA = [at(f"gate_ring{s}", KT * P, (156 + 8 * s) * K1) for s in range(2)]
    QR = at("q_rope", 2 * SEQ, 168 * K1)
    OSTAGE = at("o_staged", KT * SEQ, 136 * K1)
    GATE = at("gate_t", 4 * SEQ, 172 * K1)
    PB = [at(f"p{s}", TOK, (180 + 3 * s) * K1) for s in range(2)]
    PTS = [at(f"p_t{s}", TOK, (186 + 3 * s) * K1) for s in range(2)]
    ON = [at(f"o_nat{s}", P, 192 * K1 + 512 * s) for s in range(2)]
    GROW = at("gate_rows", D, 180 * K1, rows=2)
    CKV = at("ckv_t", 4 * TOK, 180 * K1)
    SQ1, RS1 = at("staged1", TOK, 193 * K1), at("rstd1", TOK, 196 * K1)
    XN1, TMP1 = at("normed1", TOK, 199 * K1), at("rotated1", SEQ, 202 * K1)
    TB = [at(f"nbr_bias{s}", 14 * GRID_W, 193 * K1 + 3584 * s) for s in range(2)]
    MASKS = at("masks_sb", 3 * P + CTX + GRID_W, 204 * K1)
    WIN, ZERO, COLM = MASKS[:, 0:384], MASKS[:, 384:640], MASKS[:, 640:704]
    KRR = at("k_rope_raw", TOK, 204 * K1)
    QRSQ = at("q_rope_sq", 2 * SEQ, 156 * K1)
    KR, KRSQ = at("k_rope", 2 * TOK, 0), at("k_rope_sq", TOK, 8 * K1)
    X = at("x_t", KT * SEQ, 172 * K1)
    X6 = at("x_t6", KT * TOK, 136 * K1)
    SQN, SUMN, RSN = at("staged_n", SEQ, 136 * K1), at("sq_sum", SEQ, 138 * K1), at("rstd_n", SEQ, 140 * K1)
    HF = [at(f"h_full{s}", SEQ, (142 + 2 * s) * K1) for s in range(4)]
    FIN = [at(f"final{s}", SEQ, (146 + 2 * s) * K1) for s in range(2)]
    FOUT = [at(f"final_nat{s}", SEQ, (150 + 2 * s) * K1) for s in range(2)]
    RELB, ONEH = at("rel_bias_sb", BIAS_HEADS, 97 * K1, rows=NBUCKET), at("onehot_sb", NDIST, 98 * K1, rows=NBUCKET)
    DMASK = at("dist_mask_sb", NDIST + NDIST_W, 101 * K1, rows=BIAS_HEADS)
    DTAB = at("dist_table_sb", NDIST + NDIST_W, 106 * K1, rows=BIAS_HEADS)
    Q2, IQ = at("q2_t", 8 * SEQ, 136 * K1), at("iq_t", 8 * SEQ, 152 * K1)
    K2, IK = at("k2_t", SEQ, 168 * K1), at("ik_t", SEQ, 170 * K1)
    V2 = at("v2_nat", QT * 64, 172 * K1)
    SQ2, RS2 = at("staged2", SEQ, 174 * K1), at("rstd2", SEQ, 176 * K1)
    XN2, VT2 = at("normed2", SEQ, 178 * K1), at("v2_t", SEQ, 180 * K1)
    PA = [at(f"pool_in{s}", SEQ, (182 + 2 * s) * K1) for s in range(2)]
    PS = [at(f"pool_sum{s}", SEQ, (186 + 2 * s) * K1) for s in range(2)]
    PL = [at(f"pooled{s}", SEQ, (190 + 2 * s) * K1) for s in range(4)]
    PW = at("pool_w_sb", 8 * 256, 198 * K1)
    QST = [at(f"q_stage{s}", SEQ, (182 + 2 * s) * K1) for s in range(2)]
    TRI = at("tri_sb", P, 186 * K1)
    RL = [at(f"relu{s}", SEQ, (187 + 2 * s) * K1) for s in range(2)]
    IDX, WK = at("index_score", QT * SEQ, 80 * K1), at("index_work", 3 * SEQ, 88 * K1)
    SEL = at("select_mask", 3 * SEQ, 16 * K1)
    TR = [at(f"dist_bias{s}", SEQ, (22 + 2 * s) * K1) for s in range(4)]
    TM = [at(f"masked_bias{s}", 9 * P, 30 * K1 + 4608 * s) for s in range(4)]
    P2 = [at(f"p2_{s}", SEQ, (49 + 2 * s) * K1) for s in range(2)]
    PT2 = [at(f"p2_t{s}", SEQ, (53 + 2 * s) * K1) for s in range(2)]
    ON2 = [at(f"o2_nat{s}", SEQ, (57 + 2 * s) * K1) for s in range(2)]
    Q3, K3 = at("q3_t", KT * SEQ, 136 * K1), at("k3_t", 4 * SEQ, 168 * K1)
    V3 = at("v3_nat", QT * 256, 176 * K1)
    SQ3, RS3, XN3 = at("staged3", SEQ, 180 * K1), at("rstd3", SEQ, 182 * K1), at("normed3", SEQ, 184 * K1)
    T3 = [at(f"win_bias{s}", 256, s * K1) for s in range(4)]
    P3 = [at(f"p3_{s}", 1024, (4 + 4 * s) * K1) for s in range(2)]
    PT3 = [at(f"p3_t{s}", 1024, (12 + 4 * s) * K1) for s in range(2)]
    ON3 = [at(f"o3_nat{s}", SEQ, (20 + 2 * s) * K1) for s in range(2)]
    QST3 = [at(f"q3_stage{s}", 2 * SEQ, (24 + 4 * s) * K1, rows=64) for s in range(2)]

    DST = dict(Q=Q, K=K, V=V, GATE=GATE, IQ=IQ, Q2=Q2, OT=OT, K3=K3, Q3=Q3, V3=V3)

    xt_d = [nc.dram_tensor(f"x_t_dram{n}", [KT, P, SEQ], F32, kind="Internal").ap() for n in range(3)]
    ot_d = nc.dram_tensor("o_t_dram", [KT, P, SEQ], F32, kind="Internal").ap()
    dt_d = nc.dram_tensor("dist_dram", [BIAS_HEADS, NDIST + NDIST_W], F32, kind="Internal").ap()
    sel_d = nc.dram_tensor("selection_dram", [P, 3 * SEQ], F32, kind="Internal").ap()
    dsa_d = nc.dram_tensor("dsa_bias_dram", [DSA_HEADS, P, NDIST], F32, kind="Internal").ap()
    swa_d = nc.dram_tensor("swa_bias_dram", [BIAS_HEADS, P, NDIST_W], F32, kind="Internal").ap()
    rpb_d = nc.dram_tensor("nbr_bias_dram", [GRID_W, RPB_FLAT], F32, kind="Internal").ap()

    with ExitStack() as ctx:
        ACC = ctx.enter_context(nc.psum_tensor("acc", [P, 2, 1024], F32))
        SSQ = ctx.enter_context(nc.psum_tensor("ssq", [P, 1024], F32))
        AUX = ctx.enter_context(nc.psum_tensor("aux", [P, 1024], F32))

        S = {n: ctx.enter_context(nc.semaphore(n)) for n in (
            "loaded", "nbr_spread", "dist_spread", "x_in", "rb_in", "rb_mm", "rb_tab", "rb_stored", "x_saved", "x_loaded", "o_spilled",
            "o_loaded", "raw0", "raw1", "ada0", "ada1", "ada2", "ada3", "ga0", "ga1", "nb0", "nb1", "tb0", "tb1",
            "tb2", "tb3", "out0", "out1", "rope_in", "pw_in", "tri_in",
            "x_turned", "x_copied", "x_squared", "x_summed", "x_total", "x_std", "cond_ready",
            "ada_mm", "ada_row", "ada_turned", "gate_mm", "gate_row", "gate_turned", "gate_taken",
            "hf_ready", "hf_hi", "h_ready", "h_odd", "sq_ready", "half_done", "hi_done", "lo_done", "staged", "stage_used", "sum_done",
            "std_done", "rs_done", "xn_done", "perm_done", "cos_done", "aux_free", "rope_done", "silu_done",
            "copied", "fp32_done", "resid_done", "v_side", "dve_link", "pool_link",
            "s_ready", "neg_ready", "p_ready", "t_ready", "pt_ready", "o_ready", "on_ready", "turned", "out_done",
            "bias_ready", "q_staged", "is_ready", "relu_ready", "idx_done", "sel_done", "sel_saved", "sel_loaded", "pooled", "pool_mm",
            "final_turned")}

        def need(eng, name, value):
            if isinstance(value, int) and value <= 0:
                return
            eng.wait_ge(S[name], value)

        def release(eng, rule):
            if rule:
                need(eng, rule[0], rule[1])

        def filled(eng, fill, k):
            need(eng, "h_odd" if k % 2 else "h_ready", HALF * fill + k // 2 + 1)

        def ktile(t, kt, n):
            return t[:, kt * n:(kt + 1) * n]

        def lhs(G):
            return (H1H, H1L, TOK) if G.phase == 1 else (H2H, H2L, SEQ)

        def scratch(G):
            if G.phase == 1:
                return SQ1, RS1, XN1
            return (SQN if G.kind in ("wout", "final") else SQ2, RS2, XN2) if G.phase == 2 else (SQ3, RS3, XN3)

        phase = 1
        for name, item in order:
            if name == "join":
                phase = 2 if item["fill"] < 4 else phase
            if name == "normalise" and item["layer"] == 2:
                phase = 3
            if name == "run":
                for G in item["groups"]:
                    G.phase = phase
                    if G.kind == "final":
                        G.phase = 2

        flat = [("run", G) if name == "run" else (name, None)
                for name, item in order for G in (item["groups"] if name == "run" else [None])]
        for n, (name, G) in enumerate(flat):
            if G is None:
                continue
            G.next = None
            G.primed = False
        stream = [(n, G) for n, (name, G) in enumerate(flat) if G is not None]
        for (n, G), (m, H) in zip(stream, stream[1:]):
            between = [name for name, _ in flat[n + 1:m] if name != "attend"]
            if G.split and H.split and not between:
                G.next, H.primed = H, True
        for n, (name, item) in enumerate(order):
            if name in ("start", "join", "normalise"):
                rest = [x for m, x in order[n:] if m == "run"]
                if order[n + 1][0] == "run":
                    item["first"] = rest[0]["groups"][0]
                    item["first"].primed = item["first"].whole = True

        def walk(step, flush, stages):
            prev = prev2 = None
            for name, item in order:
                if name != "run":
                    if prev is not None or prev2 is not None:
                        flush(prev, prev2)
                    prev = prev2 = None
                    if name in stages:
                        stages[name](item)
                    continue
                gs = item["groups"]
                if item.get("loop") and len(gs) >= 8:
                    stop = len(gs) if linear(gs[-1]) else len(gs) - 2
                    for G in gs[:2]:
                        step(G, prev, prev2)
                        prev, prev2 = G, prev
                    with step.eng.Fori(0, (stop - 2) // 2) as i:
                        for j in range(2):
                            moved = [gs[2 + j - b].at(2 * i, 16 * i) for b in range(3)]
                            moved[0].next = gs[3 + j].at(2 * i, 16 * i)
                            step(*moved)
                    prev, prev2 = gs[stop - 1], gs[stop - 2]
                    gs = gs[stop:]
                for G in gs:
                    step(G, prev, prev2)
                    prev, prev2 = G, prev

        def linear(G):
            N = G.next
            return N is not None and N.g == G.g + 1 and N.r == G.r + 1 and N.dmas == 1

        def ready(eng, G):
            if G.split:
                need(eng, "half_done", 2 * G.g + 2)
            else:
                need(eng, "fp32_done", G.fp32 + 1)

        def acc(G, n=None):
            return ACC[:, G.cs, 0:(n or G.n)]

        def out_of(G):
            if G.dst == "K" or G.dst == "Q":
                n = TOK if G.dst == "K" else SEQ
                return DST[G.dst][:, G.j * n:G.j * n + G.n]
            return DST[G.dst][:, bass.ds(G.j * SEQ, SEQ)]

        def gain(G):
            return COLS[:, COL[G.gain]:COL[G.gain] + 1]

        col = lambda name, j: COLS[:, bass.ds(COL[name] + j, 1)]
        cos, sin = ROPE_T[:, 0:SEQ], ROPE_T[:, SEQ:2 * SEQ]
        src_w = lambda name, c, n=P: T[name][:, bass.ds(c, n)].rearrange("(k p) c -> p k c", p=P)
        src_ada = lambda c, part: T["w_ada"][512 * part:512 * (part + 1), bass.ds(c, 512)].rearrange(
            "(k p) c -> p k c", p=P)
        tiles = lambda t, n, w=P: t[:, 0:n * w].rearrange("p (k c) -> p k c", c=w)
        U_DSA, U_SWA = 64, 128
        OUT_DSA, OUT_SWA = 64, 96
        FIRST_U = {"a": 0, "b": 16, "c": 32, "d": 48}

        def settled(eng, total, names):
            key = {"xn_done": "norm", "rope_done": "rope", "silu_done": "silu", "aux_free": "aux",
                   "copied": "copy", "stage_used": "stage", "staged": "stage", "resid_done": "resid"}
            for n in names:
                need(eng, n, total[key[n]] if n in key else total["g"] * 2)

        block = ctx.enter_context(nc.Block())

        @block.sync
        def _(sp):
            def start(item):
                for t, name in ((COLS, "cols"), (IDENT, "ident"), (ONES, "ones"), (ONES64, "ones64"),
                                (SWAP_A, "swap_a"), (SWAP_D, "swap_d"), (ROPE_T, "rope_a"), (INVC, "inv_count")):
                    sp.dma_start(t[:], T[name]).then_inc(S["loaded"], 16)
                sp.dma_start(RELB[:], T["rel_bias_2"]).then_inc(S["rb_in"], 16)
                sp.dma_start(ONEH[:], T["onehot"]).then_inc(S["rb_in"], 16)
                sp.dma_start(DMASK[:], T["dist_mask"]).then_inc(S["rb_in"], 16)
                sp.dma_start(MASKS[:], T["masks"]).then_inc(S["loaded"], 16)

                def ada(chunk, s):
                    sp.dma_start(tiles(ktile(ADAR, s, KT * P), 4, 512), src_ada(chunk * 512, s)).then_inc(S[f"ada{s}"], 16)

                for s in range(4):
                    ada(0, s)
                sp.wait_ge(S["rb_tab"], 2)
                sp.dma_start(dt_d, DTAB[:]).then_inc(S["rb_stored"], 16)
                with sp.Fori(0, 7) as i:
                    for s in range(4):
                        sp.wait_ge(S["ada_mm"], 4 * i + s + 1)
                        ada(i + 1, s)
                sp.wait_ge(S["rb_stored"], 16)
                sp.dma_start(rpb_d, bass.AP(T["rpb"].tensor, 0, [[0, GRID_W], [1, RPB_FLAT]]))\
                  .then_inc(S["nbr_spread"], 16)

            def step(G, prev, prev2):
                if not G.src:
                    return
                release(sp, G.raw_free)
                raw, sem = RAW[G.rs], S[f"raw{G.rs}"]
                name, c = G.src
                if G.kind in ("kn", "vn"):
                    sp.dma_start(tiles(raw, 4, 512), T[name].rearrange("(k p) c -> p k c", p=P)).then_inc(sem, 16)
                elif G.kind in ("qr", "kr"):
                    for b, cc in enumerate(c if G.kind == "qr" else (c, c)):
                        sp.dma_start(tiles(raw, KT)[:, :, 64 * b:64 * b + 64], src_w(name, cc, 64)).then_inc(sem, 16)
                elif G.kind == "ikw":
                    for a, cc, n in ((0, E_IK, 64), (64, E_IW, 16), (80, E_IK, 48)):
                        sp.dma_start(tiles(raw, KT)[:, :, a:a + n], src_w(name, cc, n)).then_inc(sem, 16)
                else:
                    sp.dma_start(tiles(raw, KT), src_w(name, c)).then_inc(sem, 16)
                for g in G.gate_cols:
                    if g >= 2:
                        sp.wait_ge(S["gate_mm"], g - 1)
                    else:
                        filled(sp, 0, KT - 2)
                        filled(sp, 0, KT - 1)
                    sp.dma_start(tiles(GADA[g % 2], 4, 512), src_ada(GATE_COL * P + 512 * (g // 4), g % 4))\
                      .then_inc(S[f"ga{g % 2}"], 16)

            step.eng = sp

            def diagonals(heads, tables, width, ring, used):
                w = tables.shape[2]
                for h in range(heads):
                    if h >= 4:
                        sp.wait_ge(S["neg_ready"], used(h - 4))
                    sp.dma_start(ring[h % 4][:], bass.AP(tables.tensor, h * P * w + P - 1, [[w - 1, P], [1, width]]))\
                      .then_inc(S[f"tb{h % 4}"], 16)

            def dsa(item):
                sp.wait_ge(S["half_done"], 2 * item["total"]["g"])
                sp.wait_ge(S["dist_spread"], 32)
                diagonals(DSA_HEADS, dsa_d, SEQ, TR, lambda h: U_DSA + 8 * (h // 2 + 1))

            def swa(item):
                sp.wait_ge(S["half_done"], 2 * item["total"]["g"])
                diagonals(BIAS_HEADS, swa_d, 256, T3, lambda h: U_SWA + h + 1)

            walk(step, lambda *a: None, dict(start=start, dsa=dsa, swa=swa))

        @block.scalar
        def _(act):
            A = nc.scalar

            def start(item):
                for t in range(QT):
                    act.dma_start(ktile(XNAT, t, D), T["x"][0, t * P:(t + 1) * P, :]).then_inc(S["x_in"], 16)
                for t in range(CTX // P):
                    act.dma_start(ktile(XNAT, QT + t, D), T["ctx"][0, t * P:(t + 1) * P, :]).then_inc(S["x_in"], 16)
                act.wait_ge(S["loaded"], 16 * 9)
                A.activation(CS[:], COLS[:, COL["cond"]:COL["cond"] + 32], ACT.Silu).then_inc(S["cond_ready"], 1)
                for k in range(KT):
                    act.wait_ge(S["x_copied"], k + 1)
                    if k:
                        act.wait_ge(S["x_summed"], k)
                    A.activation(SQ1[:], ktile(X6, k, TOK), ACT.Square).then_inc(S["x_squared"], 1)
                act.dma_start(xt_d[0].rearrange("k p t -> p k t"), tiles(X6, KT, TOK)[:, :, 0:SEQ])\
                   .then_inc(S["x_saved"], 16)
                act.wait_ge(S["x_total"], 1)
                act.wait_ge(S["pool_link"], 1)
                A.activation(RS1[:], SSQ[:, 0:TOK], ACT.Sqrt, bias=EPS_T[:], scale=1.0 / D).then_inc(S["x_std"], 1)
                with act.Fori(0, 4) as i:
                    for b in range(2):
                        act.wait_ge(S["ada_mm"], 8 * i + 4 * b + 4)
                        A.activation(AROW[:, bass.ds(1024 * i + 512 * b, 512)], AUX[0:2, 512 * b:512 * b + 512],
                                     ACT.Copy).then_inc(S["ada_row"], 1)
                act.wait_ge(S["ada_turned"], 1)
                for half in range(2):
                    hi(item["first"], half)
                for k in range(KT):
                    act.wait_ge(S["hf_ready"], k + 1)
                    A.activation(ktile(H1H, k, TOK), ktile(X6, k, TOK), ACT.Copy).then_inc(S["hf_hi"], 1)

            def hi(G, half):
                need(act, f"raw{G.rs}", G.landed)
                need(act, "half_done", 2 * G.g + half - 1)
                A.activation(WH[half][:], RAW[G.rs][:, half * HALF * P:(half + 1) * HALF * P],
                             ACT.Copy).then_inc(S["hi_done"], 1)

            def post(G):
                if G is None:
                    return
                SQ, RS, XN = scratch(G)
                k = G.kind
                if k in ("wout",):
                    need(act, "resid_done", G.resid + 1)
                    need(act, "sum_done", G.resid)
                    A.activation(SQN[:], X[:, bass.ds(G.j * SEQ, SEQ)], ACT.Square).then_inc(S["sq_ready"], 1)
                    return
                if k == "final":
                    return
                ready(act, G)
                if k in ("norm", "qn", "kn", "plain", "kvn", "ckv", "ikw"):
                    need(act, "stage_used", G.stage)
                if k in ("norm", "qn", "kn"):
                    A.activation(SQ[:, 0:G.n], acc(G), ACT.Square).then_inc(S["staged"], 1)
                elif k == "kvn":
                    need(act, "sel_done", 1)
                    act.dma_start(sel_d, WK[:]).then_inc(S["sel_saved"], 16)
                    A.activation(VT2[64:128, :], ACC[64:128, G.cs, 0:SEQ], ACT.Copy)
                    A.activation(SQ[:], acc(G), ACT.Square).then_inc(S["staged"], 1)
                elif k == "ckv":
                    A.activation(ktile(CKV, G.j, TOK), acc(G), ACT.Copy)
                    A.activation(SQ[:], acc(G), ACT.Square).then_inc(S["staged"], 1)
                elif k == "ikw":
                    A.activation(IK[0:64, :], ACC[0:64, G.cs, 0:SEQ], ACT.Copy)
                    A.activation(IK[64:128, :], ACC[0:64, G.cs, 0:SEQ], ACT.Copy)
                    A.activation(SQ[:], acc(G), ACT.Copy).then_inc(S["staged"], 1)
                elif k == "plain":
                    A.activation(SQ[:, 0:G.n], acc(G), ACT.Copy).then_inc(S["staged"], 1)
                elif k == "silu":
                    if G.phase == 1 and G.j == 0:
                        need(act, "o_spilled", 16 * (G.silu // 4))
                    if G.phase == 2 and G.saves:
                        need(act, "sel_saved", 16)
                    A.activation(out_of(G), acc(G), ACT.Silu).then_inc(S["silu_done"], 1)
                elif k == "copy":
                    A.activation(out_of(G), acc(G), ACT.Copy).then_inc(S["copied"], 1)
                elif k == "pin":
                    need(act, "pooled", G.j - 1)
                    A.activation(PA[G.js][:], acc(G), ACT.Copy).then_inc(S["copied"], 1)
                elif k == "qr":
                    A.activation(ktile(QR, G.j, SEQ), acc(G), ACT.Copy)
                    A.activation(ktile(QRSQ, G.j, SEQ), acc(G), ACT.Square).then_inc(S["copied"], 1)
                elif k == "kr":
                    A.activation(KRR[:], acc(G), ACT.Copy).then_inc(S["copied"], 1)
                elif k == "vn":
                    A.activation(ktile(V, G.j, 512), acc(G, 512), ACT.Copy).then_inc(S["copied"], 1)

            def std(G):
                if G is None or G.kind not in ("norm", "qn", "kn", "kvn", "ckv"):
                    return
                if G.kind == "ckv" and G.j < 3:
                    return
                SQ, RS, XN = scratch(G)
                per = {"qn": NOPE + ROPE, "kn": NOPE + ROPE, "ckv": RANK}.get(G.kind, G.per)
                need(act, "stage_used", G.stage + 1)
                need(act, "xn_done", G.norm)
                A.activation(RS[:, 0:G.n], SSQ[:, 0:G.n], ACT.Sqrt, bias=EPS_T[:], scale=1.0 / per)\
                 .then_inc(S["std_done"], 1)

            def send(G):
                if G is None or G.kind != "final":
                    return
                need(act, "aux_free", G.aux + 1)
                act.dma_start(out[0, :, bass.ds(G.j * P, P)].rearrange("(t p) c -> p t c", p=P),
                              FOUT[G.js][:].rearrange("p (t c) -> p t c", c=P)).then_inc(S[f"out{G.js}"], 16)

            def step(G, prev, prev2):
                if G.split and not G.primed:
                    hi(G, 0)
                post(prev)
                if prev is not None and prev.gate_cols and prev.gate_cols[1] % 4 == 3:
                    c = prev.gate_cols[1] // 4
                    act.wait_ge(S["gate_mm"], 4 * c + 4)
                    A.activation(GROW[:, 512 * c:512 * c + 512], AUX[0:2, 512:1024], ACT.Copy).then_inc(S["gate_row"], 1)
                if G.split and not G.whole:
                    hi(G, 1)
                std(prev)
                if G.next is not None:
                    hi(G.next, 0)
                send(prev2)

            step.eng = act

            def flush(prev, prev2):
                post(prev)
                if prev is not None and prev.gate_cols:
                    act.wait_ge(S["gate_mm"], KT)
                    A.activation(GROW[:, 3 * 512:], AUX[0:2, 512:1024], ACT.Copy).then_inc(S["gate_row"], 1)
                std(prev)
                send(prev2)
                send(prev)

            def attend(item):
                m = item["mixer"]
                U0 = FIRST_U[m]

                def nbr(h):
                    for r in range(2):
                        act.dma_start(
                            TB[h % 2][64 * r:64 * r + 64, :].rearrange("p (v c) -> p v c", c=GRID_W),
                            bass.AP(rpb_d.tensor, GRID_W + h * RPB_H * RPB_W + (1 - r) * RPB_W + 15,
                                    [[RPB_FLAT - 1, GRID_W], [RPB_W, 14], [1, GRID_W]])).then_inc(S[f"nb{h % 2}"], 16)

                def exp(n):
                    u = U0 + n
                    nk = keys(m, n % 4)
                    act.wait_ge(S["neg_ready"], u + 1)
                    c = u % 8
                    need(act, "t_ready", u - 1)
                    src = ACC[:, u % 2, 0:nk] if m in "ad" else PB[u % 2][:, 0:nk]
                    e = A.activation(PB[u % 2][:, 0:nk], src, ACT.Exp, bias=NG[:, c:c + 1],
                                     accum_out=SM[:, c:c + 1])
                    if m == "c":
                        h = n // 4
                        need(act, "on_ready", u - 7)
                        e = A.activation(ES[:, c:c + 1], NG[:, c:c + 1], ACT.Exp,
                                         bias=COLS[:, COL["c_sink"] + h:COL["c_sink"] + h + 1])
                    e.then_inc(S["p_ready"], 1)

                w = NDIST + NDIST_W
                if m == "a":
                    act.wait_ge(S["rb_stored"], 16)
                    act.dma_start(dsa_d, bass.AP(dt_d.tensor, 0, [[w, DSA_HEADS], [0, P], [1, NDIST]]))\
                       .then_inc(S["dist_spread"], 16)
                if m == "c":
                    act.dma_start(swa_d, bass.AP(dt_d.tensor, NDIST, [[w, BIAS_HEADS], [0, P], [1, NDIST_W]]))\
                       .then_inc(S["dist_spread"], 16)
                if m == "b":
                    act.wait_ge(S["nbr_spread"], 16)
                    settled(act, item["total"], ("xn_done", "rope_done", "stage_used", "aux_free"))
                    nbr(0)
                    nbr(1)
                exp(0)
                for n in range(16):
                    u = U0 + n
                    nk = keys(m, n % 4)
                    act.wait_ge(S["t_ready"], u + 1)
                    need(act, "o_ready", u - 1)
                    A.activation(PTS[u % 2][:, 0:nk], SSQ[:, 0:nk], ACT.Copy).then_inc(S["pt_ready"], 1)
                    if n < 15:
                        exp(n + 1)
                    if m == "b" and n in (4, 8):
                        act.wait_ge(S["neg_ready"], U0 + n)
                        nbr(n // 4 + 1)
                act.wait_ge(S["out_done"], U0 + 16)
                i = "abcd".index(m)
                act.dma_start(ot_d[4 * i:4 * i + 4].rearrange("k p t -> p k t"), tiles(GATE, 4, SEQ))\
                   .then_inc(S["o_spilled"], 16)
                if m == "c":
                    act.dma_start(ROPE_T[:], T["rope_d"]).then_inc(S["rope_in"], 16)

            def latent(item):
                act.wait_ge(S["half_done"], 2 * item["total"]["g"])
                A.activation(KRSQ[:], KRR[:], ACT.Square).then_inc(S["v_side"], 1)

            def join(item):
                f, t = item["fill"], item["total"]
                act.wait_ge(S["half_done"], 2 * t["g"])
                n = (f - 1) // 2
                if f == 1:
                    act.wait_ge(S["o_spilled"], 64)
                    act.dma_start(tiles(OSTAGE, KT, SEQ), ot_d.rearrange("k p t -> p k t")).then_inc(S["o_loaded"], 16)
                act.dma_start(tiles(X, KT, SEQ), xt_d[n].rearrange("k p t -> p k t")).then_inc(S["x_loaded"], 16)
                if f == 1:
                    act.wait_ge(S["o_loaded"], 16)
                for half in range(2):
                    hi(item["first"], half)
                for k in range(KT):
                    A.activation(ktile(H2H, k, SEQ), ktile(OSTAGE if f == 1 else OT, k, SEQ), ACT.Copy)\
                     .then_inc(S["hf_hi"], 1)

            HF_BEFORE = {2: KT, 4: 2 * KT}

            def normalise(item):
                f, t = item["fill"], item["total"]
                settled(act, t, ("resid_done", "half_done"))
                act.dma_start(xt_d[item["layer"]].rearrange("k p t -> p k t"), tiles(X, KT, SEQ))\
                   .then_inc(S["x_saved"], 16)
                for half in range(2):
                    hi(item["first"], half)
                act.wait_ge(S["x_total"], 1 + item["layer"])
                A.activation(RSN[:], SSQ[:, 0:SEQ], ACT.Sqrt, bias=EPS_T[:], scale=1.0 / D).then_inc(S["x_std"], 1)
                for k in range(KT):
                    act.wait_ge(S["hf_ready"], HF_BEFORE[f] + k + 1)
                    A.activation(ktile(H2H, k, SEQ), HF[k % 4][:], ACT.Copy).then_inc(S["hf_hi"], 1)
                act.wait_ge(S["x_saved"], 16 * (1 + item["layer"]))
                if item["layer"] == 1:
                    act.dma_start(tiles(PW, 8, 256), T["pool_w"].rearrange("g (k p) d -> p (g k) d", p=P))\
                       .then_inc(S["pw_in"], 16)

            def index(item):
                settled(act, item["total"], ("aux_free", "half_done", "silu_done"))
                act.dma_start(TRI[:], T["tri"]).then_inc(S["tri_in"], 16)
                with act.Fori(0, 4) as i:
                    for n in range(16):
                        x = 16 * i + n
                        qt, slot = n % 4, n % 4
                        nk = P * (qt + 1)
                        act.wait_ge(S["is_ready"], x + 1)
                        act.wait_ge(S["idx_done"], x + 1)
                        A.activation(RL[n % 2][:, 0:nk], ACC[:, slot // 2, (slot % 2) * 512:(slot % 2) * 512 + nk],
                                     ACT.Relu).then_inc(S["relu_ready"], 1)

            def dsa(item):
                def exp(i, n):
                    qt, u = (n // 2) % 4, U_DSA + 16 * i + n
                    nk, c = P * (qt + 1), n % 8
                    act.wait_ge(S["neg_ready"], u + 1)
                    A.activation(P2[n % 2][:, 0:nk], P2[n % 2][:, 0:nk], ACT.Exp, bias=NG[:, c:c + 1],
                                 accum_out=SM[:, c:c + 1]).then_inc(S["p_ready"], 1)

                def body(i, last):
                    for n in range(16):
                        qt, u = (n // 2) % 4, U_DSA + 16 * i + n
                        nk = P * (qt + 1)
                        act.wait_ge(S["t_ready"], u + 1)
                        act.wait_ge(S["o_ready"], u - 1)
                        A.activation(PT2[n % 2][:, 0:nk], SSQ[:, 0:nk], ACT.Copy).then_inc(S["pt_ready"], 1)
                        if n < 15:
                            exp(i, n + 1)
                        elif not last:
                            exp(i + 1, 0)

                exp(0, 0)
                with act.Fori(0, 3) as i:
                    body(i, False)
                body(3, True)
                act.wait_ge(S["out_done"], OUT_SWA)

            def swa(item):
                def exp(i, n):
                    u = U_SWA + 8 * i + n
                    c = 4 * (n % 2)
                    act.wait_ge(S["neg_ready"], u + 1)
                    act.wait_ge(S["on_ready"], u - 1)
                    for t in range(QT):
                        a, b = (P if t == 0 else 256 * t), 256 * (t + 1)
                        A.activation(P3[n % 2][:, a:b], P3[n % 2][:, a:b], ACT.Exp, bias=NG[:, c + t:c + t + 1],
                                     accum_out=SM[:, c + t:c + t + 1])
                    A.activation(ES[:, c:c + 4], NG[:, c:c + 4], ACT.Exp, bias=col("o_sink", 8 * i + n))\
                     .then_inc(S["p_ready"], 1)

                def body(i, last):
                    for n in range(8):
                        u = U_SWA + 8 * i + n
                        act.wait_ge(S["t_ready"], u + 1)
                        act.wait_ge(S["o_ready"], u - 1)
                        A.activation(PT3[n % 2][:, 0:7 * P], SSQ[:, 0:7 * P], ACT.Copy).then_inc(S["pt_ready"], 1)
                        if n < 7:
                            exp(i, n + 1)
                        elif not last:
                            exp(i + 1, 0)

                exp(0, 0)
                with act.Fori(0, 3) as i:
                    body(i, False)
                body(3, True)
                act.wait_ge(S["out_done"], OUT_SWA + 16)

            def end(item):
                for s in range(2):
                    act.wait_ge(S[f"out{s}"], 16 * 8)

            walk(step, flush, dict(start=start, attend=attend, latent=latent, join=join, normalise=normalise,
                                   index=index, dsa=dsa, swa=swa, end=end))

        @block.gpsimd
        def _(pool):
            G_ = nc.gpsimd

            def start(item):
                G_.memset(EPS_T[:], EPS).then_inc(S["pool_link"], 1)
                for k in range(KT):
                    pool.wait_ge(S["x_squared"], k + 1)
                    if k == 0:
                        G_.tensor_copy(XN1[:], SQ1[:]).then_inc(S["x_summed"], 1)
                    else:
                        pool.wait_ge(S["x_summed"], k)
                        G_.tensor_tensor(XN1[:], XN1[:], SQ1[:], ALU.add).then_inc(S["x_summed"], 1)
                for half in range(2):
                    lo(item["first"], half)
                for k in range(0, KT, 2):
                    pool.wait_ge(S["hf_hi"], k + 1)
                    G_.tensor_tensor(ktile(H1L, k, TOK), ktile(X6, k, TOK), ktile(H1H, k, TOK).bitcast(F32),
                                     ALU.subtract).then_inc(S["h_ready"], 1)

            def lo(G, half):
                need(pool, "hi_done", 2 * G.g + half + 1)
                G_.tensor_tensor(WL[half][:], RAW[G.rs][:, half * HALF * P:(half + 1) * HALF * P],
                                 WH[half][:].bitcast(F32), ALU.subtract).then_inc(S["lo_done"], 1)

            def side(G):
                if G is None:
                    return
                if G.kind == "norm" and G.rotate:
                    need(pool, "xn_done", G.norm + 1)
                    if G.n > SEQ:
                        G_.tensor_copy(out_of(G)[:, SEQ:G.n], XN1[:, SEQ:G.n])
                    G_.tensor_tensor(out_of(G)[:, 0:SEQ], XN1[:, 0:SEQ], cos, ALU.mult).then_inc(S["cos_done"], 1)
                if G.kind == "wout":
                    need(pool, "sq_ready", G.resid + 1)
                    need(pool, "pool_link", 2 + G.layer)
                    need(pool, "sum_done", G.resid)
                    G_.tensor_tensor(SUMN[:], SUMN[:], SQN[:], ALU.add).then_inc(S["sum_done"], 1)

            def step(G, prev, prev2):
                if G.split:
                    if not G.primed:
                        lo(G, 0)
                    if not G.whole:
                        lo(G, 1)
                    if G.next is not None:
                        lo(G.next, 0)
                side(prev)

            step.eng = pool

            def attend(item):
                m = item["mixer"]
                U0 = FIRST_U[m]
                if m == "b":
                    for h in range(4):
                        tb = TB[h % 2][:].rearrange("p (v c) -> p v c", c=GRID_W)
                        pool.wait_ge(S[f"nb{h % 2}"], 32 * (h // 2 + 1))
                        G_.tensor_tensor(tb, tb, COLM.unsqueeze(1).to_broadcast([P, 14, GRID_W]), ALU.add)\
                          .then_inc(S["bias_ready"], 1)
                pool.wait_ge(S["out_done"], U0 + 16)

            def lo_parts(src, base):
                for k in range(0, KT, 2):
                    pool.wait_ge(S["hf_hi"], base + k + 1)
                    G_.tensor_tensor(ktile(H2L, k, SEQ), src(k), ktile(H2H, k, SEQ).bitcast(F32),
                                     ALU.subtract).then_inc(S["h_ready"], 1)

            def join(item):
                f = item["fill"]
                for half in range(2):
                    lo(item["first"], half)
                lo_parts(lambda k: ktile(OSTAGE if f == 1 else OT, k, SEQ), KT * f)
                if f < 5:
                    filled(pool, f, KT - 2)
                    filled(pool, f, KT - 1)
                    G_.memset(SUMN[:], 0.0).then_inc(S["pool_link"], 1)

            def normalise(item):
                f = item["fill"]
                for half in range(2):
                    lo(item["first"], half)
                lo_parts(lambda k: HF[k % 4][:], KT * f)
                pool.wait_ge(S["x_saved"], 16 * (1 + item["layer"]))

            def index(item):
                settled(pool, item["total"], ("copied",))

                def copy(i, s, first):
                    if not first:
                        pool.wait_ge(S["is_ready"], 8 * (2 * i + s - 1))
                    G_.tensor_copy(QST[s][:], IQ[:, bass.ds((2 * i + s) * SEQ, SEQ)]).then_inc(S["q_staged"], 1)

                for s in range(2):
                    copy(0, s, True)
                with pool.Fori(1, 4) as i:
                    for s in range(2):
                        copy(i, s, False)

            def dsa(item):
                def masked(i, n):
                    h = 4 * i + n
                    pool.wait_ge(S[f"tb{n}"], 16 * i + 16)
                    pool.wait_ge(S["neg_ready"], U_DSA + 8 * (2 * i + n // 2 - 1))
                    at0 = 0
                    for qt in range(1, QT):
                        nk = P * (qt + 1)
                        e = G_.tensor_tensor(TM[n][:, at0:at0 + nk], TR[n][:, SEQ - nk:SEQ],
                                             SEL[:, (qt - 1) * SEQ:(qt - 1) * SEQ + nk], ALU.add)
                        at0 += nk
                    e.then_inc(S["bias_ready"], 1)

                def copy(i, s):
                    pool.wait_ge(S["s_ready"], U_DSA + 8 * (2 * i + s - 1))
                    G_.tensor_copy(QST[s][:], Q2[:, bass.ds((2 * i + s) * SEQ, SEQ)]).then_inc(S["q_staged"], 1)

                pool.wait_ge(S["half_done"], 2 * item["total"]["g"])
                pool.wait_ge(S["pooled"], 8)
                pool.wait_ge(S["xn_done"], item["total"]["norm"])
                pool.dma_start(SEL[:], sel_d).then_inc(S["sel_loaded"], 16)
                pool.wait_ge(S["sel_loaded"], 16)
                with pool.Fori(0, 4) as i:
                    for s in range(2):
                        copy(i, s)
                        masked(i, 2 * s)
                        masked(i, 2 * s + 1)
                pool.wait_ge(S["out_done"], OUT_SWA)

            def swa(item):
                def copy(i, s):
                    pool.wait_ge(S["s_ready"], U_SWA + 2 * (2 * i + s - 1))
                    for half in range(2):
                        e = G_.tensor_copy(QST3[s][:, half * SEQ:(half + 1) * SEQ],
                                           Q3[64 * half:64 * half + 64, bass.ds((2 * i + s) * SEQ, SEQ)])
                    e.then_inc(S["q_staged"], 1)

                settled(pool, item["total"], ("xn_done", "half_done"))
                with pool.Fori(0, 8) as i:
                    for s in range(2):
                        copy(i, s)
                pool.wait_ge(S["out_done"], OUT_SWA + 16)

            walk(step, lambda prev, prev2: side(prev), dict(start=start, attend=attend, join=join,
                                                             normalise=normalise, index=index, dsa=dsa, swa=swa))

        @block.vector
        def _(dve):
            Vv = nc.vector
            L = Links(dve, S["dve_link"])

            def start(item):
                dve.wait_ge(S["loaded"], 16 * 9)
                for name, d in (("a_q", HEAD), ("b_q", HEAD), ("c_q", HEAD), ("d_qn", 192), ("d_qr", 192),
                                ("e_q", 64), ("o_q", 64)):
                    c = COLS[:, COL[name]:COL[name] + 1]
                    L.done(Vv.tensor_scalar(c, c, float(d) ** -0.5, None, ALU.mult))
                dve.wait_ge(S["rb_in"], 48)
                dve.wait_ge(S["rb_mm"], 1)
                Vv.tensor_tensor(DTAB[:, 0:NDIST], SSQ[0:BIAS_HEADS, 0:NDIST], DMASK[:, 0:NDIST],
                                 ALU.add).then_inc(S["rb_tab"], 1)
                Vv.tensor_tensor(DTAB[:, NDIST:NDIST + NDIST_W], SSQ[0:BIAS_HEADS, NDIST - NDIST_W:NDIST],
                                 DMASK[:, NDIST:NDIST + NDIST_W], ALU.add).then_inc(S["rb_tab"], 1)
                for k in range(KT):
                    dve.wait_ge(S["x_turned"], k + 1)
                    Vv.tensor_copy(ktile(X6, k, TOK), ACC[:, k % 2, 0:TOK]).then_inc(S["x_copied"], 1)
                dve.wait_ge(S["x_std"], 1)
                L.link(Vv.reciprocal(RS1[:], RS1[:]))
                dve.wait_ge(S["x_saved"], 16)
                for k in range(KT):
                    L.done(Vv.tensor_tensor(ktile(X6, k, TOK), ktile(X6, k, TOK), RS1[:], ALU.mult))
                dve.wait_ge(S["ada_turned"], 1)
                ada = ADA[:].rearrange("p (g b) -> p g b", b=2)
                two = lambda name, first, n: COLS[:, COL[name] + first:COL[name] + first + n].unsqueeze(2)\
                    .to_broadcast([P, n, 2])
                L.link(Vv.tensor_tensor(ada[:, 0:2 * KT], ACC[:, 0, 0:4 * KT].rearrange("p (g b) -> p g b", b=2),
                                        two("b_ada", 0, 2 * KT), ALU.add))
                L.link(Vv.tensor_scalar(ada[:, KT:2 * KT], ada[:, KT:2 * KT], 1.0, None, ALU.add))
                L.link(Vv.tensor_tensor(ada[:, KT:2 * KT], ada[:, KT:2 * KT], two("norm_g", 0, KT), ALU.mult))
                for k in range(KT):
                    for b, (a, z) in enumerate(((0, SEQ), (SEQ, TOK))):
                        part = X6[:, k * TOK + a:k * TOK + z]
                        e = Vv.tensor_scalar(part, part, ADA[:, 2 * (KT + k) + b:2 * (KT + k) + b + 1],
                                             ADA[:, 2 * k + b:2 * k + b + 1], ALU.mult, ALU.add)
                    e.then_inc(S["hf_ready"], 1)
                    if k % 2 and k > 2:
                        lo_part(0, k - 2, ktile(X6, k - 2, TOK), H1H, H1L, TOK)
                lo_part(0, KT - 1, ktile(X6, KT - 1, TOK), H1H, H1L, TOK)

            def lo_part(fill, k, full, hi_t, lo_t, n):
                dve.wait_ge(S["hf_hi"], KT * fill + k + 1)
                Vv.tensor_tensor(ktile(lo_t, k, n), full, ktile(hi_t, k, n).bitcast(F32),
                                 ALU.subtract).then_inc(S["h_odd"], 1)

            def join(item):
                f = item["fill"]
                for k in range(1, KT, 2):
                    lo_part(f, k, ktile(OSTAGE if f == 1 else OT, k, SEQ), H2H, H2L, SEQ)

            def side(G):
                if G is None:
                    return
                if G.kind == "plain":
                    need(dve, "stage_used", G.stage + 1)
                    nt = G.n // P
                    dst = (VA if G.width == 256 and G.phase == 1 else DST[G.dst])
                    Vv.tensor_copy(tiles(dst, nt, G.width)[:, :, G.j * P:(G.j + 1) * P], tiles(AUX, nt))\
                      .then_inc(S["aux_free"], 1)
                if G.kind == "ikw":
                    need(dve, "stage_used", G.stage + 1)
                    Vv.tensor_scalar(IW[:], AUX[:, 0:64], 1.0 / 32, None, ALU.mult).then_inc(S["aux_free"], 1)
                if G.kind == "kvn":
                    need(dve, "stage_used", G.stage + 1)
                    Vv.tensor_copy(V2[:], AUX[:, 0:QT * 64]).then_inc(S["aux_free"], 1)

            def norm(G):
                if G is None:
                    return
                k = G.kind
                if k == "wout":
                    ready(dve, G)
                    need(dve, "x_loaded", 16 * (G.layer + 1))
                    xj = X[:, bass.ds(G.j * SEQ, SEQ)]
                    if G.layer == 0:
                        Vv.scalar_tensor_tensor(out=xj, in0=acc(G), scalar=ADA[:, bass.ds(2 * (GATE_COL + G.j), 1)],
                                                in1=xj, op0=ALU.mult, op1=ALU.add).then_inc(S["resid_done"], 1)
                    else:
                        Vv.tensor_tensor(xj, acc(G), xj, ALU.add).then_inc(S["resid_done"], 1)
                    return
                if k == "final":
                    ready(dve, G)
                    need(dve, "x_loaded", 48)
                    need(dve, "final_turned", G.j - 1)
                    Vv.tensor_tensor(FIN[G.js][:], acc(G), X[:, bass.ds(G.j * SEQ, SEQ)], ALU.add)\
                      .then_inc(S["resid_done"], 1)
                    return
                if k == "pin":
                    return pool_group(G)
                if k not in ("norm", "qn", "kn", "kvn", "ckv") or (k == "ckv" and G.j < 3):
                    return
                SQ, RS, XN = scratch(G)
                RS = RS[:, 0:G.n]
                need(dve, "std_done", G.norm + 1)
                Vv.reciprocal(RS, RS).then_inc(S["rs_done"], 1)
                need(dve, "rs_done", G.norm + 1)
                if k == "norm" and G.rotate:
                    need(dve, "rope_done", G.rope)
                    Vv.scalar_tensor_tensor(out=XN[:, 0:G.n], in0=acc(G), scalar=gain(G), in1=RS, op0=ALU.mult,
                                            op1=ALU.mult).then_inc(S["xn_done"], 1)
                elif k == "norm" and G.dst == "K3":
                    L.link(Vv.scalar_tensor_tensor(out=XN[:], in0=acc(G), scalar=gain(G), in1=RS, op0=ALU.mult,
                                                   op1=ALU.mult))
                    for h in range(2):
                        for half in range(2):
                            e = Vv.tensor_copy(K3[64 * half:64 * half + 64, (2 * G.j + h) * SEQ:(2 * G.j + h + 1) * SEQ],
                                               XN[64 * h:64 * h + 64, :])
                    e.then_inc(S["xn_done"], 1)
                    need(dve, "xn_done", G.norm + 1)
                elif k == "norm":
                    Vv.scalar_tensor_tensor(out=out_of(G), in0=acc(G), scalar=gain(G), in1=RS, op0=ALU.mult,
                                            op1=ALU.mult).then_inc(S["xn_done"], 1)
                elif k == "kvn":
                    for half in range(2):
                        e = Vv.scalar_tensor_tensor(out=K2[64 * half:64 * half + 64, :], in0=ACC[0:64, G.cs, 0:SEQ],
                                                    scalar=gain(G)[0:64], in1=RS[0:64, :], op0=ALU.mult, op1=ALU.mult)
                    e.then_inc(S["xn_done"], 1)
                elif k in ("qn", "kn"):
                    Vv.scalar_tensor_tensor(out=out_of(G), in0=acc(G), scalar=gain(G), in1=RS, op0=ALU.mult,
                                            op1=ALU.mult)
                    rows = slice(64 * (G.j % 2), 64 * (G.j % 2) + 64)
                    if k == "qn":
                        src = dst = ktile(QR, G.j // 2, SEQ)[rows]
                        g = COLS[rows, COL["d_qr"]:COL["d_qr"] + 1]
                    else:
                        src, dst = KRR[rows, :], ktile(KR, G.j // 2, TOK)[rows]
                        g = COLS[rows, COL["d_kr"]:COL["d_kr"] + 1]
                    Vv.scalar_tensor_tensor(out=dst, in0=src, scalar=g, in1=RS[rows, :], op0=ALU.mult,
                                            op1=ALU.mult).then_inc(S["xn_done"], 1)
                else:
                    for j in range(4):
                        c = ktile(CKV, j, TOK)
                        e = Vv.scalar_tensor_tensor(out=c, in0=c, scalar=COLS[:, COL["d_kv"] + j:COL["d_kv"] + j + 1],
                                                    in1=RS, op0=ALU.mult, op1=ALU.mult)
                    e.then_inc(S["xn_done"], 1)

            def rotate(G):
                if G is None or not G.rotate:
                    return
                TMP = TMP1[:]
                need(dve, "rope_in", 16 if G.kind in ("qn", "kn") else 0)
                need(dve, "perm_done", G.rope + 1)
                Vv.tensor_tensor(TMP, AUX[:, 0:SEQ], sin, ALU.mult).then_inc(S["aux_free"], 1)
                need(dve, "aux_free", G.aux + 1)
                if G.kind == "norm":
                    dst = out_of(G)[:, 0:SEQ]
                    need(dve, "cos_done", G.rope + 1)
                else:
                    dst = ktile(QR, G.j // 2, SEQ) if G.kind == "qn" else ktile(KR, G.j // 2, TOK)[:, 0:SEQ]
                    L.link(Vv.tensor_tensor(dst, dst, cos, ALU.mult))
                Vv.tensor_tensor(dst, dst, TMP, ALU.add).then_inc(S["rope_done"], 1)
                need(dve, "rope_done", G.rope + 1)

            def pool_group(G):
                w = G.j // 2
                need(dve, "copied", G.copy + 1)
                a, n = PA[G.js], 1
                src = a
                for step_ in range(w + 1):
                    dst = PS[step_ % 2]
                    L.done(Vv.tensor_copy(dst[:, 0:n], src[:, 0:n]))
                    L.link(Vv.tensor_tensor(dst[:, n:SEQ], src[:, n:SEQ], src[:, 0:SEQ - n], ALU.add))
                    src, n = dst, 2 * n
                pl = PL[G.j % 4]
                need(dve, "pool_mm", (G.j - 2) // 2)
                L.link(Vv.tensor_tensor(src[:, 0:16], src[:, 0:16], INVC[:, 16 * w:16 * w + 16], ALU.mult))
                Vv.tensor_tensor(pl[:, 0:16], src[:, 0:16], a[:, 0:16], ALU.subtract)
                Vv.scalar_tensor_tensor(out=pl[:, 16:SEQ], in0=src[:, 16:SEQ], scalar=1.0 / POOL_WINDOWS[w],
                                        in1=a[:, 16:SEQ], op0=ALU.mult, op1=ALU.subtract).then_inc(S["pooled"], 1)
                need(dve, "pooled", G.j + 1)

            def pool_out(G):
                if G is None or G.kind != "pin" or G.j % 2 == 0:
                    return
                need(dve, "pool_mm", G.j // 2 + 1)
                for b in range(2):
                    j = G.j - 1 + b
                    o = ktile(OT, j, SEQ)
                    Vv.scalar_tensor_tensor(out=o, in0=AUX[:, b * 512:(b + 1) * 512],
                                            scalar=COLS[:, COL["pool_scale"] + j:COL["pool_scale"] + j + 1],
                                            in1=o, op0=ALU.mult, op1=ALU.mult).then_inc(S["aux_free"], 1)

            def final_out(G):
                if G is None or G.kind != "final":
                    return
                need(dve, "final_turned", G.j + 1)
                need(dve, f"out{G.js}", 8 * (G.j - G.js))
                Vv.tensor_copy(FOUT[G.js][:], AUX[:, 0:SEQ]).then_inc(S["aux_free"], 1)

            def late(G):
                rotate(G)
                pool_out(G)
                final_out(G)

            def step(G, prev, prev2):
                late(prev2)
                side(prev)
                norm(prev)

            step.eng = dve

            def flush(prev, prev2):
                late(prev2)
                side(prev)
                norm(prev)
                late(prev)

            def masked_max(psum, bias, pb, first, c, c2):
                return Vv.tensor_tensor_reduce(out=pb, in0=psum, in1=bias, scale=1.0, scalar=first, op0=ALU.add,
                                               op1=ALU.max, accum_out=MX[:, c2:c2 + 1])

            def attend(item):
                m = item["mixer"]
                U0 = FIRST_U[m]
                settled(dve, item["total"], ("silu_done",))
                if m == "a":
                    dve.wait_ge(S["gate_turned"], 1)
                    n = 2 * KT
                    Vv.tensor_tensor(ADA[:, 4 * KT:6 * KT].rearrange("p (g b) -> p g b", b=2),
                                     AUX[:, 640:640 + n].rearrange("p (g b) -> p g b", b=2),
                                     COLS[:, COL["b_ada"] + 2 * KT:COL["b_ada"] + 3 * KT].unsqueeze(2)
                                     .to_broadcast([P, KT, 2]), ALU.add).then_inc(S["gate_taken"], 1)

                def maxima(n):
                    u, h, qt = U0 + n, n // 4, n % 4
                    c, s = u % 8, ACC[:, u % 2, :]
                    pb = PB[u % 2]
                    dve.wait_ge(S["s_ready"], u + 1)
                    if m in "ad":
                        Vv.tensor_reduce(NG[:, c:c + 1], s[:, 0:TOK], AX, ALU.max, negate=True)\
                          .then_inc(S["neg_ready"], 1)
                        return
                    need(dve, "t_ready", u - 1)
                    if m == "b":
                        dve.wait_ge(S["bias_ready"], h + 1)
                        a = (6 - 2 * qt) * GRID_W
                        L.link(masked_max(s[:, 0:SEQ], TB[h % 2][:, a:a + SEQ], pb[:, 0:SEQ], NEG, c, c))
                        lat, first = SEQ, NEG
                    else:
                        lat = keys(m, qt) - CTX
                        a = P if qt == 0 else 0
                        sink = COLS[:, COL["c_sink"] + h:COL["c_sink"] + h + 1]
                        L.link(masked_max(s[:, 0:lat], WIN[:, a:a + lat], pb[:, 0:lat], sink, c, c))
                    L.link(masked_max(s[:, lat:lat + CTX], ZERO, pb[:, lat:lat + CTX], MX[:, c:c + 1], c, (c + 4) % 8))
                    Vv.tensor_scalar(NG[:, c:c + 1], MX[:, (c + 4) % 8:(c + 4) % 8 + 1], -1.0, None, ALU.mult)\
                      .then_inc(S["neg_ready"], 1)

                def finish(n):
                    u, h, qt = U0 + n, n // 4, n % 4
                    dve.wait_ge(S["turned"], u + 1)
                    g = GATE[:, h * SEQ + qt * P:h * SEQ + (qt + 1) * P]
                    Vv.tensor_tensor(g, AUX[:, 512:512 + P], g, ALU.mult).then_inc(S["out_done"], 1)

                maxima(0)
                for n in range(16):
                    u = U0 + n
                    c = u % 8
                    if n < 15:
                        maxima(n + 1)
                    if n:
                        finish(n - 1)
                    dve.wait_ge(S["p_ready"], u + 1)
                    if m == "c":
                        L.link(Vv.tensor_tensor(SM[:, c:c + 1], SM[:, c:c + 1], ES[:, c:c + 1], ALU.add))
                    L.link(Vv.reciprocal(RI[:, c:c + 1], SM[:, c:c + 1]))
                    dve.wait_ge(S["o_ready"], u + 1)
                    need(dve, "turned", u - 1)
                    Vv.tensor_scalar(ON[u % 2][:], AUX[:, 0:P], RI[:, c:c + 1], None, ALU.mult)\
                      .then_inc(S["on_ready"], 1)
                finish(15)
                dve.wait_ge(S["out_done"], U0 + 16)

            HF_BEFORE = {2: KT, 4: 2 * KT}

            def normalise(item):
                f, layer = item["fill"], item["layer"]
                g = COL["even_norm" if layer == 1 else "odd_norm"]
                dve.wait_ge(S["x_std"], 1 + layer)
                L.link(Vv.reciprocal(RSN[:], RSN[:]))
                for k in range(KT):
                    if k >= 4:
                        filled(dve, f, k - 4)
                    Vv.scalar_tensor_tensor(out=HF[k % 4][:], in0=ktile(X, k, SEQ), scalar=COLS[:, g + k:g + k + 1],
                                            in1=RSN[:], op0=ALU.mult, op1=ALU.mult).then_inc(S["hf_ready"], 1)
                    if k % 2 and k > 2:
                        lo_part(f, k - 2, HF[(k - 2) % 4][:], H2H, H2L, SEQ)
                lo_part(f, KT - 1, HF[(KT - 1) % 4][:], H2H, H2L, SEQ)
                dve.wait_ge(S["x_saved"], 16 * (1 + layer))
                filled(dve, f, KT - 2)
                filled(dve, f, KT - 1)

            def index(item):
                Vv.memset(IDX[:], 0.0).then_inc(S["idx_done"], 2)
                with dve.Fori(0, 4) as i:
                    for n in range(16):
                        x, qt = 16 * i + n, n % 4
                        nk = P * (qt + 1)
                        sc = IDX[:, qt * SEQ:qt * SEQ + nk]
                        dve.wait_ge(S["relu_ready"], x + 1)
                        dve.wait_ge(S["idx_done"], x - 1 if n >= 4 else x + 2)
                        Vv.scalar_tensor_tensor(out=sc, in0=RL[n % 2][:, 0:nk],
                                                scalar=IW[:, bass.ds(qt * 16 + 4 * i + n // 4, 1)], in1=sc,
                                                op0=ALU.mult, op1=ALU.add).then_inc(S["idx_done"], 1)
                dve.wait_ge(S["idx_done"], 66)
                dve.wait_ge(S["tri_in"], 16)
                for t in range(3):
                    d = IDX[:, (t + 1) * SEQ + (t + 1) * P:(t + 1) * SEQ + (t + 2) * P]
                    L.done(Vv.tensor_tensor(d, d, TRI[:], ALU.add))
                L.wait()
                L.done(Vv.memset(WK[:, P * 2:SEQ], 0.0))
                L.done(Vv.memset(WK[:, SEQ + P * 3:2 * SEQ], 0.0))
                wk = [WK[:, t * SEQ:t * SEQ + P * (t + 2)] for t in range(3)]
                for t in range(3):
                    L.done(Vv.tensor_copy(wk[t], IDX[:, (t + 1) * SEQ:(t + 1) * SEQ + P * (t + 2)]))
                L.wait()
                for _round in range(TOPK // 8):
                    for t in range(3):
                        L.done(Vv.max(M8[:, 8 * t:8 * t + 8], wk[t]))
                    L.wait()
                    for t in range(3):
                        L.done(Vv.match_replace(wk[t], M8[:, 8 * t:8 * t + 8], wk[t], -3.0e38))
                    L.wait()
                for t in range(3):
                    L.done(Vv.tensor_tensor(wk[t], wk[t], IDX[:, (t + 1) * SEQ:(t + 1) * SEQ + P * (t + 2)],
                                            ALU.is_equal))
                L.wait()
                for t in range(3):
                    e = Vv.tensor_scalar(wk[t], wk[t], NEG, None, ALU.mult)
                e.then_inc(S["sel_done"], 1)

            def dsa(item):
                def maxima(i, n):
                    qt, half, pair = (n // 2) % 4, n % 2, n // 8
                    u, c = U_DSA + 16 * i + n, n % 8
                    nk, slot = P * (qt + 1), 2 * pair + half
                    dve.wait_ge(S["s_ready"], u + 1)
                    dve.wait_ge(S["t_ready"], u - 1)
                    at0 = (0, 0, 2 * P, 5 * P)[qt]
                    if qt == 0:
                        dve.wait_ge(S["bias_ready"], 4 + 4 * i + slot + 1)
                    bias = TR[slot][:, SEQ - nk:SEQ] if qt == 0 else TM[slot][:, at0:at0 + nk]
                    pb = P2[n % 2][:, 0:nk]
                    L.link(Vv.tensor_tensor(pb, ACC[:, n % 2, 0:nk], bias, ALU.add))
                    Vv.tensor_reduce(NG[:, c:c + 1], pb, AX, ALU.max, negate=True).then_inc(S["neg_ready"], 1)

                def finish(i, n):
                    qt, pair = (n // 2) % 4, n // 8
                    dve.wait_ge(S["turned"], OUT_DSA + 8 * i + (n + 1) // 2)
                    g = OT[:, bass.ds((8 + 2 * i + pair) * SEQ + qt * P, P)]
                    Vv.tensor_tensor(g, AUX[:, 512:512 + P], g, ALU.mult).then_inc(S["out_done"], 1)

                def body(i, last):
                    for n in range(16):
                        half, c = n % 2, n % 8
                        u = U_DSA + 16 * i + n
                        if n < 15:
                            maxima(i, n + 1)
                        elif not last:
                            maxima(i + 1, 0)
                        if n and half == 0:
                            finish(i, n - 1)
                        dve.wait_ge(S["p_ready"], u + 1)
                        L.link(Vv.reciprocal(RI[:, c:c + 1], SM[:, c:c + 1]))
                        dve.wait_ge(S["o_ready"], u + 1)
                        dve.wait_ge(S["turned"], OUT_DSA + 8 * i + n // 2 - 1)
                        Vv.tensor_scalar(ON2[(n // 2) % 2][:, half * 64:half * 64 + 64], AUX[:, 0:64],
                                         RI[:, c:c + 1], None, ALU.mult).then_inc(S["on_ready"], 1)
                    finish(i, 15)

                settled(dve, item["total"], ("half_done", "silu_done"))
                maxima(0, 0)
                with dve.Fori(0, 3) as i:
                    L.enter(i, 32)
                    body(i, False)
                L.leave(3)
                body(3, True)
                dve.wait_ge(S["out_done"], OUT_SWA)

            def swa(item):
                def maxima(i, n):
                    u, c = U_SWA + 8 * i + n, 4 * (n % 2)
                    dve.wait_ge(S["s_ready"], u + 1)
                    dve.wait_ge(S["t_ready"], u - 1)
                    dve.wait_ge(S[f"tb{n % 4}"], 64 + 32 * i + 16 * (n // 4) + 16)
                    pb, bias = P3[n % 2], T3[n % 4]
                    own, rest = slice(P, 256), lambda t: t[:, 256:1024].rearrange("p (t k) -> p t k", k=256)
                    L.done(Vv.tensor_tensor(pb[:, own], ACC[:, n % 2, own], bias[:, own], ALU.add))
                    L.link(Vv.tensor_tensor(rest(pb), rest(ACC[:, n % 2, :]), bias[:].unsqueeze(1).to_broadcast([P, 3, 256]),
                                            ALU.add))
                    L.done(Vv.tensor_reduce(MX[:, c:c + 1], pb[:, own], AX, ALU.max))
                    L.link(Vv.tensor_reduce(MX[:, c + 1:c + 4], rest(pb), AX, ALU.max))
                    Vv.tensor_scalar(NG[:, c:c + 4], MX[:, c:c + 4], col("o_sink", 8 * i + n), -1.0, ALU.max, ALU.mult)\
                      .then_inc(S["neg_ready"], 1)

                def finish(i, n):
                    dve.wait_ge(S["turned"], OUT_SWA + 4 * i + (n + 1) // 2)
                    g = OT[:, bass.ds((4 * i + n // 2) * SEQ, SEQ)]
                    Vv.tensor_tensor(g, AUX[:, 512:1024], g, ALU.mult).then_inc(S["out_done"], 1)

                def body(i, last):
                    for n in range(8):
                        half, c = n % 2, 4 * (n % 2)
                        u = U_SWA + 8 * i + n
                        if n < 7:
                            maxima(i, n + 1)
                        elif not last:
                            maxima(i + 1, 0)
                        if n and half == 0:
                            finish(i, n - 1)
                        dve.wait_ge(S["p_ready"], u + 1)
                        L.link(Vv.tensor_tensor(SM[:, c:c + 4], SM[:, c:c + 4], ES[:, c:c + 4], ALU.add))
                        L.link(Vv.reciprocal(RI[:, c:c + 4], SM[:, c:c + 4]))
                        dve.wait_ge(S["o_ready"], u + 1)
                        dve.wait_ge(S["turned"], OUT_SWA + 4 * i + n // 2 - 1)
                        Vv.tensor_tensor(tiles(ON3[n // 2 % 2], QT)[:, :, half * 64:half * 64 + 64],
                                         tiles(AUX, QT, 64), RI[:, c:c + 4].unsqueeze(2).to_broadcast([P, QT, 64]),
                                         ALU.mult).then_inc(S["on_ready"], 1)
                    finish(i, 7)

                maxima(0, 0)
                with dve.Fori(0, 3) as i:
                    L.enter(i, 48)
                    body(i, False)
                L.leave(3)
                body(3, True)
                dve.wait_ge(S["out_done"], OUT_SWA + 16)

            walk(step, flush, dict(start=start, attend=attend, join=join, normalise=normalise, index=index, dsa=dsa,
                                   swa=swa))

        @block.tensor
        def _(pe):
            M = nc.tensor

            def mm(out_, lhsT, rhs, start, stop):
                return M.matmul(out_, lhsT, rhs, start=start, stop=stop, skip_group_check=True)

            def turn(out_, in_, rows=slice(0, P)):
                return M.transpose(out_, in_, IDENT[rows, rows])

            def ada_piece(dst, weights, part):
                for k4 in range(4):
                    k = 4 * part + k4
                    e = mm(dst, CS[:, 2 * k:2 * k + 2], ktile(weights, k4, 512), k == 0, k == KT - 1)
                return e

            def start(item):
                pe.wait_ge(S["loaded"], 16 * 9)
                pe.wait_ge(S["rb_in"], 48)
                for a, b in spans(NDIST):
                    e = mm(SSQ[0:BIAS_HEADS, a:b], RELB[:], ONEH[:, a:b], True, True)
                e.then_inc(S["rb_mm"], 1)
                pe.wait_ge(S["x_in"], 16 * 6)
                for k in range(KT):
                    if k >= 2:
                        pe.wait_ge(S["x_copied"], k - 1)
                    for t in range(TOK // P):
                        e = turn(ACC[:, k % 2, t * P:(t + 1) * P], XNAT[:, t * D + k * P:t * D + (k + 1) * P])
                    e.then_inc(S["x_turned"], 1)
                pe.wait_ge(S["cond_ready"], 1)

                def chunk(i, b, peeled):
                    if not peeled:
                        pe.wait_ge(S["ada_row"], 2 * i + b - 1)
                    for s in range(4):
                        pe.wait_ge(S[f"ada{s}"], 32 * i + 16 * b + 16)
                        ada_piece(AUX[0:2, 512 * b:512 * b + 512], ktile(ADAR, s, KT * P), s).then_inc(S["ada_mm"], 1)

                for b in range(2):
                    chunk(0, b, True)
                pe.wait_ge(S["rb_tab"], 2)
                pe.wait_ge(S["x_summed"], KT)
                for a, b in spans(TOK):
                    e = mm(SSQ[:, a:b], ONES[:], XN1[:, a:b], True, True)
                e.then_inc(S["x_total"], 1)
                with pe.Fori(1, 4) as i:
                    for b in range(2):
                        chunk(i, b, False)
                pe.wait_ge(S["ada_row"], 8)
                pe.wait_ge(S["x_copied"], KT)
                for g in range(2 * KT):
                    e = turn(ACC[:, 0, 2 * g:2 * g + 2], AROW[:, g * P:(g + 1) * P], slice(0, 2))
                e.then_inc(S["ada_turned"], 1)
                pe.wait_ge(S["x_std"], 1)
                pe.wait_ge(S["hf_ready"], 1)

            def first(G):
                if G is None:
                    return
                SQ, RS, XN = scratch(G)
                k = G.kind
                if k in ("norm", "qn", "kn", "kvn", "ckv"):
                    need(pe, "staged", G.stage + 1)
                    if k != "ckv" or G.j == 0:
                        need(pe, "std_done", G.norm)
                    if k == "kn":
                        need(pe, "v_side", 1)
                    if k == "kvn":
                        need(pe, "aux_free", G.aux)
                    own = ONES64 if G.ones == "ones64" else ONES
                    for a, b in spans(G.n):
                        more = k in ("qn", "kn")
                        e = mm(SSQ[:, a:b], own[:], SQ[:, a:b], k != "ckv" or G.j == 0,
                               (G.j == 3) if k == "ckv" else not more)
                        if more:
                            rows = slice(64 * (G.j % 2), 64 * (G.j % 2) + 64)
                            sq = ktile(QRSQ, G.j // 2, SEQ) if k == "qn" else KRSQ
                            e = mm(SSQ[:, a:b], ONES[rows, :], sq[rows, a:b], False, True)
                    if k == "kvn":
                        for t in range(QT):
                            e = turn(AUX[:, t * 64:(t + 1) * 64], VT2[64:128, t * P:(t + 1) * P], slice(64, 128))
                    e.then_inc(S["stage_used"], 1)
                elif k == "plain":
                    need(pe, "staged", G.stage + 1)
                    need(pe, "aux_free", G.aux)
                    for t in range(G.n // P):
                        e = turn(AUX[:, t * P:(t + 1) * P], SQ[:, t * P:(t + 1) * P])
                    e.then_inc(S["stage_used"], 1)
                elif k == "ikw":
                    need(pe, "staged", G.stage + 1)
                    need(pe, "aux_free", G.aux)
                    for t in range(QT):
                        e = turn(AUX[:, t * 16:(t + 1) * 16], SQ[64:80, t * P:(t + 1) * P], slice(64, 80))
                    e.then_inc(S["stage_used"], 1)

            def second(G):
                if G is None:
                    return
                if G.rotate:
                    need(pe, "xn_done", G.norm + 1)
                    need(pe, "aux_free", G.aux)
                    src, swap = {"norm": lambda: (XN1[:, 0:SEQ], SWAP_A),
                                 "qn": lambda: (ktile(QR, G.j // 2, SEQ), SWAP_D),
                                 "kn": lambda: (ktile(KR, G.j // 2, TOK)[:, 0:SEQ], SWAP_D)}[G.kind]()
                    mm(AUX[:, 0:SEQ], swap[:], src, True, True).then_inc(S["perm_done"], 1)
                if G.kind == "pin" and G.j % 2:
                    need(pe, "pooled", G.j + 1)
                    need(pe, "aux_free", G.aux)
                    need(pe, "pw_in", 16)
                    for b in range(2):
                        for ct in range(2):
                            at_ = (G.j - 1 + ct) * 256 + b * P
                            e = mm(AUX[:, b * 512:(b + 1) * 512], PW[:, at_:at_ + P], PL[(G.j - 1 + ct) % 4][:],
                                   ct == 0, ct == 1)
                    e.then_inc(S["pool_mm"], 1)
                if G.kind == "final":
                    need(pe, "resid_done", G.resid + 1)
                    need(pe, "aux_free", G.aux)
                    for t in range(QT):
                        e = turn(AUX[:, t * P:(t + 1) * P], FIN[G.js][:, t * P:(t + 1) * P])
                    e.then_inc(S["final_turned"], 1)

            def step(G, prev, prev2):
                release(pe, G.acc_free)
                if G.kind == "kn":
                    w = G.weights
                    need(pe, f"raw{w.rs}", w.landed)
                    for k in range(RANK // P):
                        for a, b in spans(TOK):
                            e = mm(acc(G)[:, a:b], RAW[w.rs][:, k * 512 + G.j * P:k * 512 + (G.j + 1) * P],
                                   CKV[:, k * TOK + a:k * TOK + b], k == 0, k == 3)
                    e.then_inc(S["fp32_done"], 1)
                    first(prev)
                elif G.kind == "vn":
                    w = G.weights
                    need(pe, f"raw{w.rs}", w.landed)
                    for k in range(RANK // P):
                        e = mm(acc(G, 512), CKV[:, k * TOK + G.j * P:k * TOK + (G.j + 1) * P], ktile(RAW[w.rs], k, 512),
                               k == 0, k == 3)
                    e.then_inc(S["fp32_done"], 1)
                    first(prev)
                else:
                    hh, hl, n = lhs(G)
                    for half in range(2):
                        need(pe, "lo_done", 2 * G.g + half + 1)
                        for k8 in range(HALF):
                            k = half * HALF + k8
                            if G.fill is not None:
                                filled(pe, G.fill, k)
                            w = (ktile(WH[half], k8, P), ktile(WL[half], k8, P))
                            for m, (wt, ht) in enumerate(((w[0], hh), (w[0], hl), (w[1], hh))):
                                for a, b in spans(G.n):
                                    e = mm(acc(G)[:, a:b], wt, ht[:, k * n + a:k * n + b],
                                           k == 0 and m == 0, k == KT - 1 and m == 2)
                            if half == 0 and k8 == 2:
                                first(prev)
                        e.then_inc(S["half_done"], 1)
                second(prev)
                for g in G.gate_cols:
                    if g == 0:
                        need(pe, "aux_free", G.gate_after)
                    elif g % 4 == 0:
                        pe.wait_ge(S["gate_row"], g // 4)
                    pe.wait_ge(S[f"ga{g % 2}"], 16 * (g // 2 + 1))
                    ada_piece(AUX[0:2, 512:1024], GADA[g % 2], g % 4).then_inc(S["gate_mm"], 1)

            step.eng = pe

            def flush(prev, prev2):
                first(prev)
                second(prev)

            def attend(item):
                m = item["mixer"]
                U0 = FIRST_U[m]
                settled(pe, item["total"], ("xn_done", "rope_done", "silu_done", "aux_free", "copied"))
                if m == "a":
                    pe.wait_ge(S["gate_row"], 4)
                    for g in range(KT):
                        e = turn(AUX[:, 640 + 2 * g:642 + 2 * g], GROW[:, g * P:(g + 1) * P], slice(0, 2))
                    e.then_inc(S["gate_turned"], 1)
                    pe.wait_ge(S["gate_taken"], 1)
                vv, width = (VA, 256) if m in "ac" else (V, 512)

                def scores(n):
                    u, h, qt = U0 + n, n // 4, n % 4
                    kv = h // 2 if m in "ac" else h
                    need(pe, "p_ready", u - 1)
                    q = Q[:, h * SEQ + qt * P:h * SEQ + (qt + 1) * P]
                    lo_key, hi_key = (0, SEQ) if m != "c" else (max(0, qt - 1) * P, min(SEQ, (qt + 2) * P))
                    parts, at_ = [], 0
                    for a, b in ((lo_key, hi_key), (SEQ, TOK)):
                        while a < b:
                            w = min(b - a, 512 - at_ % 512)
                            parts.append((at_, a, w))
                            at_, a = at_ + w, a + w
                    for c, key, w in parts:
                        dst = ACC[:, u % 2, c:c + w]
                        e = mm(dst, q, K[:, kv * TOK + key:kv * TOK + key + w], True, m != "d")
                        if m == "d":
                            rows = slice(64 * (h % 2), 64 * (h % 2) + 64)
                            e = mm(dst, ktile(QR, h // 2, SEQ)[rows, qt * P:(qt + 1) * P],
                                   ktile(KR, h // 2, TOK)[rows, key:key + w], False, True)
                    e.then_inc(S["s_ready"], 1)

                def out_turn(n):
                    u = U0 + n
                    pe.wait_ge(S["on_ready"], u + 1)
                    need(pe, "out_done", u)
                    turn(AUX[:, 512:512 + P], ON[u % 2][:]).then_inc(S["turned"], 1)

                scores(0)
                scores(1)
                for n in range(16):
                    u, h, qt = U0 + n, n // 4, n % 4
                    nb = keys(m, qt) // P
                    pe.wait_ge(S["p_ready"], u + 1)
                    need(pe, "pt_ready", u)
                    for b in range(nb):
                        e = turn(SSQ[:, b * P:(b + 1) * P], PB[u % 2][:, b * P:(b + 1) * P])
                    e.then_inc(S["t_ready"], 1)
                    if n < 14:
                        scores(n + 2)
                    if n:
                        out_turn(n - 1)
                    pe.wait_ge(S["pt_ready"], u + 1)
                    need(pe, "on_ready", u)
                    kv = h // 2 if m in "ac" else h
                    lat0 = 0 if m != "c" else max(0, qt - 1)
                    for b in range(nb):
                        tile = lat0 + b if b < nb - 2 else QT + b - (nb - 2)
                        e = mm(AUX[:, 0:P], PTS[u % 2][:, b * P:(b + 1) * P],
                               vv[:, tile * width + kv * P:tile * width + (kv + 1) * P], b == 0, b == nb - 1)
                    e.then_inc(S["o_ready"], 1)
                out_turn(15)
                pe.wait_ge(S["out_done"], U0 + 16)

            def latent(item):
                settled(pe, item["total"], ("xn_done",))

            def normalise(item):
                need(pe, "sum_done", item["total"]["resid"])
                mm(SSQ[:, 0:SEQ], ONES[:], SUMN[:], True, True).then_inc(S["x_total"], 1)
                pe.wait_ge(S["x_std"], 1 + item["layer"])

            def index(item):
                settled(pe, item["total"], ("copied", "aux_free", "xn_done", "silu_done", "staged"))
                with pe.Fori(0, 4) as i:
                    for n in range(16):
                        pair, half, qt = n // 8, (n // 4) % 2, n % 4
                        nk, rows = P * (qt + 1), slice(64 * half, 64 * half + 64)
                        x = 16 * i + n
                        if n % 8 == 0:
                            pe.wait_ge(S["q_staged"], 2 * i + pair + 1)
                        if n >= 4:
                            pe.wait_ge(S["relu_ready"], x - 3)
                        else:
                            pe.wait_ge(S["idx_done"], x + 1)
                        mm(ACC[:, qt // 2, (qt % 2) * 512:(qt % 2) * 512 + nk], QST[pair][rows, qt * P:(qt + 1) * P],
                           IK[rows, 0:nk], True, True).then_inc(S["is_ready"], 1)
                pe.wait_ge(S["relu_ready"], 64)

            def dsa(item):
                settled(pe, item["total"], ("copied", "aux_free", "xn_done", "silu_done", "staged"))

                def scores(i, n):
                    pair, qt, half = n // 8, (n // 2) % 4, n % 2
                    nk, rows = P * (qt + 1), slice(64 * half, 64 * half + 64)
                    if n % 8 == 0:
                        pe.wait_ge(S["q_staged"], 8 + 2 * i + pair + 1)
                    pe.wait_ge(S["p_ready"], U_DSA + 16 * i + n - 1)
                    mm(ACC[:, n % 2, 0:nk], QST[pair][rows, qt * P:(qt + 1) * P], K2[rows, 0:nk], True, True)\
                        .then_inc(S["s_ready"], 1)

                def out_turn(i, n):
                    pe.wait_ge(S["on_ready"], U_DSA + 16 * i + n + 1)
                    pe.wait_ge(S["out_done"], OUT_DSA + 8 * i + n // 2)
                    turn(AUX[:, 512:512 + P], ON2[(n // 2) % 2][:, 0:P]).then_inc(S["turned"], 1)

                def body(i, last):
                    for n in range(16):
                        qt, half, u = (n // 2) % 4, n % 2, U_DSA + 16 * i + n
                        pe.wait_ge(S["p_ready"], u + 1)
                        pe.wait_ge(S["pt_ready"], u)
                        for b in range(qt + 1):
                            e = turn(SSQ[:, b * P:(b + 1) * P], P2[n % 2][:, b * P:(b + 1) * P])
                        e.then_inc(S["t_ready"], 1)
                        if n < 14:
                            scores(i, n + 2)
                        elif not last:
                            scores(i + 1, n - 14)
                        if n and half == 0:
                            out_turn(i, n - 1)
                        pe.wait_ge(S["pt_ready"], u + 1)
                        pe.wait_ge(S["on_ready"], u)
                        for b in range(qt + 1):
                            e = mm(AUX[:, 0:64], PT2[n % 2][:, b * P:(b + 1) * P], V2[:, b * 64:(b + 1) * 64],
                                   b == 0, b == qt)
                        e.then_inc(S["o_ready"], 1)
                    out_turn(i, 15)

                scores(0, 0)
                scores(0, 1)
                with pe.Fori(0, 3) as i:
                    body(i, False)
                body(3, True)
                pe.wait_ge(S["out_done"], OUT_SWA)

            def swa(item):
                settled(pe, item["total"], ("copied", "aux_free", "xn_done", "silu_done"))

                def scores(i, n):
                    pair, half = n // 2, n % 2
                    for t in range(QT):
                        a, b = (P if t == 0 else 256 * t), 256 * (t + 1)
                        key = i * SEQ + max(0, t - 1) * P
                        e = mm(ACC[:, n % 2, a:b], QST3[pair % 2][:, half * SEQ + t * P:half * SEQ + (t + 1) * P],
                               K3[0:64, bass.ds(key, b - a)], True, True)
                    e.then_inc(S["s_ready"], 1)

                def queries(i, n):
                    if n % 2 == 0:
                        pe.wait_ge(S["q_staged"], 16 + 4 * i + n // 2 + 1)

                def out_turn(i, n):
                    pe.wait_ge(S["on_ready"], U_SWA + 8 * i + n + 1)
                    pe.wait_ge(S["out_done"], OUT_SWA + 4 * i + n // 2)
                    for t in range(QT):
                        e = turn(AUX[:, 512 + t * P:512 + (t + 1) * P], ON3[n // 2 % 2][:, t * P:(t + 1) * P])
                    e.then_inc(S["turned"], 1)

                def body(i, last):
                    for n in range(8):
                        half, u = n % 2, U_SWA + 8 * i + n
                        if n < 6:
                            queries(i, n + 2)
                        elif not last:
                            queries(i + 1, n - 6)
                        pe.wait_ge(S["p_ready"], u + 1)
                        pe.wait_ge(S["pt_ready"], u)
                        for b in range(7):
                            e = turn(SSQ[:, b * P:(b + 1) * P], P3[n % 2][:, (b + 1) * P:(b + 2) * P])
                        e.then_inc(S["t_ready"], 1)
                        if n < 6:
                            scores(i, n + 2)
                        elif not last:
                            scores(i + 1, n - 6)
                        if n and half == 0:
                            out_turn(i, n - 1)
                        pe.wait_ge(S["pt_ready"], u + 1)
                        pe.wait_ge(S["on_ready"], u)
                        for t in range(QT):
                            tiles_ = [(0, 0)] if t == 0 else [(2 * t - 1, t - 1), (2 * t, t)]
                            for m, (b, key) in enumerate(tiles_):
                                e = mm(AUX[:, 64 * t:64 * t + 64], PT3[n % 2][:, b * P:(b + 1) * P],
                                       V3[:, bass.ds(key * 256 + i * 64, 64)], m == 0, m == len(tiles_) - 1)
                        e.then_inc(S["o_ready"], 1)
                    out_turn(i, 7)

                queries(0, 0)
                pe.wait_ge(S["p_ready"], U_SWA)
                scores(0, 0)
                scores(0, 1)
                with pe.Fori(0, 3) as i:
                    body(i, False)
                body(3, True)
                pe.wait_ge(S["out_done"], OUT_SWA + 16)

            walk(step, flush, dict(start=start, attend=attend, latent=latent, normalise=normalise, index=index,
                                   dsa=dsa, swa=swa))


def kernel(**inputs):
    import numpy as _np
    import concourse.bacc as _bacc
    from concourse import mybir as _mybir
    from concourse.bass_utils import run_bass_kernel_spmd as _run

    a = {n: _np.asarray(v) for n, v in inputs.items()}
    arrays = {n: _np.ascontiguousarray(a[n]) for n in ("x", "ctx", "rel_bias_2")}
    for to, of in (("w_ada", "w_ada"), ("w_in", "w_in"), ("w_out", "w_out"), ("w_uk", "d_w_uk"), ("w_uv", "d_w_uv"),
                   ("even_w_in", "even_w_in_2"), ("even_w_out", "even_w_out_2"), ("pool_w", "even_pool_w_2"),
                   ("odd_w_in", "odd_w_in_2"), ("odd_w_out", "odd_w_out_2")):
        arrays[to] = _np.ascontiguousarray(a[of][0])
    tall = lambda v: v.reshape(-1, P).T
    twice = lambda v: _np.concatenate([v, v])[:, None]
    wide = lambda v: _np.broadcast_to(v[None, :], (P, v.size))
    cond = _np.stack([tall(a["c"][0]), tall(a["c_ctx"])], axis=2).reshape(P, 2 * KT)
    cols = {"norm_g": tall(a["norm_g"][0]), "b_ada": tall(a["b_ada"][0]), "cond": cond,
            "even_norm": tall(a["even_norm_2"][0]), "odd_norm": tall(a["odd_norm_2"][0]),
            "pool_scale": tall(a["even_pool_scale_2"][0]),
            "a_q": a["a_q_g"].T, "a_k": a["a_k_g"].T, "b_q": a["b_q_g"].T, "b_k": a["b_k_g"].T,
            "c_q": a["c_q_g"].T, "c_k": a["c_k_g"].T, "d_kv": tall(a["d_kv_g"][0]),
            "d_qn": a["d_q_g"][:, :NOPE].T, "d_qr": twice(a["d_q_g"][0, NOPE:]),
            "d_kn": a["d_k_g"][:, :NOPE].T, "d_kr": twice(a["d_k_g"][0, NOPE:]),
            "e_q": twice(a["even_q_gain_2"][0]), "e_k": twice(a["even_k_gain_2"][0]),
            "o_q": twice(a["odd_q_gain_2"][0]), "o_k": twice(a["odd_k_gain_2"][0]),
            "c_sink": wide(a["c_sink"][0]), "o_sink": wide(a["odd_sinks_2"][0])}
    arrays["cols"] = _np.ascontiguousarray(_np.concatenate([cols[n] for n, _ in COL_LIST], axis=1))
    arrays["rpb"] = _np.pad(a["b_rpb"].reshape(1, -1), ((0, 0), (GRID_W, GRID_W)))
    arrays.update(shape_constants())

    nc = _bacc.Bacc("TRN2", target_bir_lowering=False, num_devices=1)
    T = {n: nc.dram_tensor(f"in_{n}", v.shape, _mybir.dt.from_np(v.dtype), kind="ExternalInput").ap()
         for n, v in arrays.items()}
    out = nc.dram_tensor("out_0", (1, SEQ, D), _mybir.dt.float32, kind="ExternalOutput").ap()
    build(nc, T, out)
    r = _run(nc, [{f"in_{n}": v for n, v in arrays.items()}], core_ids=[0])
    return r.results[0]["out_0"]
```
